# Optimizing a Trainium2 kernel written in Bass

```python
import jax, jax.numpy as jnp
from jax import lax
import numpy as np

D_MODEL = 2048
BATCH = 1
SEQ = 256
DEPTH = 2

HEAD_DIM = 128
FOX_HEADS = 8
DSA_HEADS = 8
IDX_HEADS = 16
IDX_DIM = 64
IDX_TOPK_MAX = 256
SWA_HEADS = 32
SWA_KV_HEADS = 4
SWA_HEAD_DIM = 64
SWA_WINDOW = 128
Q_BLOCK = 128
DSA_Q_BLOCK = 64
ROPE_THETA = 10000.0
EPS = 1e-6
NEG = -1e30

FOX_W = FOX_HEADS * HEAD_DIM
DSA_W = DSA_HEADS * HEAD_DIM
SWA_W = SWA_HEADS * SWA_HEAD_DIM
SWA_KV_W = SWA_KV_HEADS * SWA_HEAD_DIM
EVEN_SPLITS = [FOX_W, FOX_W, FOX_W, FOX_W, FOX_HEADS,
               DSA_W, DSA_W, DSA_W, DSA_W,
               IDX_HEADS * IDX_DIM, IDX_DIM, IDX_HEADS]
EVEN_IN = sum(EVEN_SPLITS)
ODD_SPLITS = [SWA_W, SWA_KV_W, SWA_KV_W, SWA_W]
ODD_IN = sum(ODD_SPLITS)
N_EVEN = (DEPTH + 1) // 2
N_ODD = DEPTH // 2

kernel_name = "hybrid_fox_dsa_swa_gated"

def rmsnorm(x, g):
    xf = x.astype(jnp.float32)
    y = xf * lax.rsqrt(jnp.mean(xf * xf, axis=-1, keepdims=True) + EPS)
    return (y * g.astype(jnp.float32)).astype(x.dtype)

def split_cols(h, sizes):
    return jnp.split(h, np.cumsum(sizes)[:-1].tolist(), axis=-1)

def rope_tables(seq, dim):
    inv = 1.0 / (ROPE_THETA ** (jnp.arange(0, dim, 2, dtype=jnp.float32) / dim))
    ang = jnp.arange(seq, dtype=jnp.float32)[:, None] * inv[None, :]
    return jnp.cos(ang), jnp.sin(ang)

def apply_rope(x, cos, sin):
    x1, x2 = jnp.split(x.astype(jnp.float32), 2, axis=-1)
    c = cos[None, :, None, :]
    s = sin[None, :, None, :]
    return jnp.concatenate([x1 * c - x2 * s, x1 * s + x2 * c], axis=-1).astype(x.dtype)

def fox_attention(q, k, v, log_f):
    B, S, H, D = q.shape
    nb = S // Q_BLOCK
    c = jnp.cumsum(log_f, axis=1).transpose(0, 2, 1)
    qb = q.reshape(B, nb, Q_BLOCK, H, D).transpose(1, 0, 2, 3, 4)
    cb = c.reshape(B, H, nb, Q_BLOCK).transpose(2, 0, 1, 3)
    kpos = jnp.arange(S)
    scale = D ** -0.5

    def block(args):
        i, qi, ci = args
        qpos = i * Q_BLOCK + jnp.arange(Q_BLOCK)
        s = jnp.einsum('bqhd,bkhd->bhqk', qi, k).astype(jnp.float32) * scale
        s = s + ci[..., None] - c[:, :, None, :]
        s = jnp.where((kpos[None, :] <= qpos[:, None])[None, None], s, NEG)
        p = jax.nn.softmax(s, axis=-1)
        return jnp.einsum('bhqk,bkhd->bqhd', p.astype(v.dtype), v)

    out = lax.map(block, (jnp.arange(nb), qb, cb))
    return out.transpose(1, 0, 2, 3, 4).reshape(B, S, H, D)

def dsa_attention(q, k, v, iq, ik, iw, topk):
    B, S, H, D = q.shape
    nb = S // DSA_Q_BLOCK
    qb = q.reshape(B, nb, DSA_Q_BLOCK, H, D).transpose(1, 0, 2, 3, 4)
    iqb = iq.reshape(B, nb, DSA_Q_BLOCK, IDX_HEADS, IDX_DIM).transpose(1, 0, 2, 3, 4)
    iwb = iw.reshape(B, nb, DSA_Q_BLOCK, IDX_HEADS).transpose(1, 0, 2, 3)
    kpos = jnp.arange(S)
    gather = jax.vmap(lambda xb, ib: xb[ib])

    def block(args):
        i, qi, iqi, iwi = args
        qpos = i * DSA_Q_BLOCK + jnp.arange(DSA_Q_BLOCK)
        logits = jnp.einsum('bqhd,bkd->bqhk', iqi, ik).astype(jnp.float32) * IDX_DIM ** -0.5
        score = jnp.einsum('bqh,bqhk->bqk', iwi.astype(jnp.float32), jax.nn.relu(logits))
        score = jnp.where((kpos[None, :] <= qpos[:, None])[None], score, NEG)
        _, idx = lax.top_k(score, topk)
        valid = idx <= qpos[None, :, None]
        ks = gather(k, idx)
        vs = gather(v, idx)
        s = jnp.einsum('bqhd,bqkhd->bhqk', qi, ks).astype(jnp.float32) * D ** -0.5
        s = jnp.where(valid[:, None], s, NEG)
        p = jax.nn.softmax(s, axis=-1)
        return jnp.einsum('bhqk,bqkhd->bqhd', p.astype(v.dtype), vs)

    out = lax.map(block, (jnp.arange(nb), qb, iqb, iwb))
    return out.transpose(1, 0, 2, 3, 4).reshape(B, S, H, D)

def swa_attention(q, k, v, sinks):
    B, S, HQ, D = q.shape
    HKV = k.shape[2]
    G = HQ // HKV
    W = SWA_WINDOW
    nb = S // W
    qb = q.reshape(B, nb, W, HKV, G, D)

    def band(t):
        tb = t.reshape(B, nb, W, HKV, D)
        prev = jnp.pad(tb, ((0, 0), (1, 0), (0, 0), (0, 0), (0, 0)))[:, :-1]
        return jnp.concatenate([prev, tb], axis=2)

    kb, vb = band(k), band(v)
    s = jnp.einsum('bnqhgd,bnkhd->bnhgqk', qb, kb).astype(jnp.float32) * D ** -0.5
    kpos = jnp.arange(2 * W)[None, :]
    rel = (jnp.arange(W)[:, None] + W) - kpos
    mask = (rel >= 0) & (rel < W)
    mask = mask[None] & ((jnp.arange(nb)[:, None, None] > 0) | (kpos >= W)[None])
    s = jnp.where(mask[None, :, None, None], s, NEG)
    sink = jnp.broadcast_to(sinks.reshape(HKV, G).astype(jnp.float32)[None, None, :, :, None, None],
                            s.shape[:-1] + (1,))
    p = jax.nn.softmax(jnp.concatenate([s, sink], axis=-1), axis=-1)[..., :-1]
    o = jnp.einsum('bnhgqk,bnkhd->bnqhgd', p.astype(v.dtype), vb)
    return o.reshape(B, S, HQ, D)

def even_layer(x, g_norm, w_in, b_f, g_qk_fox, g_qk_dsa, g_kidx, w_out, rope128, rope64, topk):
    B, S, _ = x.shape
    h = rmsnorm(x, g_norm) @ w_in
    aq, ak, av, ag, af, bq, bk, bv, bg, iq, ik, iw = split_cols(h, EVEN_SPLITS)
    aq = rmsnorm(aq.reshape(B, S, FOX_HEADS, HEAD_DIM), g_qk_fox[0])
    ak = rmsnorm(ak.reshape(B, S, FOX_HEADS, HEAD_DIM), g_qk_fox[1])
    log_f = jax.nn.log_sigmoid((af + b_f).astype(jnp.float32))
    ya = fox_attention(aq, ak, av.reshape(B, S, FOX_HEADS, HEAD_DIM), log_f)
    ya = ya.reshape(B, S, FOX_W) * jax.nn.silu(ag)
    bq = apply_rope(rmsnorm(bq.reshape(B, S, DSA_HEADS, HEAD_DIM), g_qk_dsa[0]), *rope128)
    bk = apply_rope(rmsnorm(bk.reshape(B, S, DSA_HEADS, HEAD_DIM), g_qk_dsa[1]), *rope128)
    iq = apply_rope(iq.reshape(B, S, IDX_HEADS, IDX_DIM), *rope64)
    ik = apply_rope(rmsnorm(ik, g_kidx)[:, :, None, :], *rope64)[:, :, 0]
    iw = iw * IDX_HEADS ** -0.5
    yb = dsa_attention(bq, bk, bv.reshape(B, S, DSA_HEADS, HEAD_DIM), iq, ik, iw, topk)
    yb = yb.reshape(B, S, DSA_W) * jax.nn.silu(bg)
    return x + jnp.concatenate([ya, yb], axis=-1) @ w_out

def odd_layer(x, g_norm, w_in, g_qk, sinks, w_out, rope64):
    B, S, _ = x.shape
    h = rmsnorm(x, g_norm) @ w_in
    q, k, v, g = split_cols(h, ODD_SPLITS)
    q = apply_rope(rmsnorm(q.reshape(B, S, SWA_HEADS, SWA_HEAD_DIM), g_qk[0]), *rope64)
    k = apply_rope(rmsnorm(k.reshape(B, S, SWA_KV_HEADS, SWA_HEAD_DIM), g_qk[1]), *rope64)
    v = v.reshape(B, S, SWA_KV_HEADS, SWA_HEAD_DIM)
    y = swa_attention(q, k, v, sinks).reshape(B, S, SWA_W) * jax.nn.silu(g)
    return x + y @ w_out

def setup_inputs(seed: int = 0) -> dict:
    key = jax.random.key(seed)
    ks = jax.random.split(key, 13)
    nrm = lambda k, shape, s: jax.random.normal(k, shape, jnp.float32) * s
    gain = lambda k, shape: 1.0 + 0.02 * jax.random.normal(k, shape, jnp.float32)
    return {
        "x": nrm(ks[0], (BATCH, SEQ, D_MODEL), 1.0),
        "norm_even": gain(ks[1], (N_EVEN, D_MODEL)),
        "w_in_even": nrm(ks[2], (N_EVEN, D_MODEL, EVEN_IN), D_MODEL ** -0.5),
        "b_f_even": nrm(ks[3], (N_EVEN, FOX_HEADS), 0.1),
        "g_qk_fox": gain(ks[4], (N_EVEN, 2, HEAD_DIM)),
        "g_qk_dsa": gain(ks[5], (N_EVEN, 2, HEAD_DIM)),
        "g_kidx": gain(ks[6], (N_EVEN, IDX_DIM)),
        "w_out_even": nrm(ks[7], (N_EVEN, FOX_W + DSA_W, D_MODEL), (FOX_W + DSA_W) ** -0.5),
        "norm_odd": gain(ks[8], (N_ODD, D_MODEL)),
        "w_in_odd": nrm(ks[9], (N_ODD, D_MODEL, ODD_IN), D_MODEL ** -0.5),
        "g_qk_swa": gain(ks[10], (N_ODD, 2, SWA_HEAD_DIM)),
        "sinks": nrm(ks[11], (N_ODD, SWA_HEADS), 0.5),
        "w_out_odd": nrm(ks[12], (N_ODD, SWA_W, D_MODEL), SWA_W ** -0.5),
    }

def reference(x, norm_even, w_in_even, b_f_even, g_qk_fox, g_qk_dsa, g_kidx, w_out_even,
              norm_odd, w_in_odd, g_qk_swa, sinks, w_out_odd):
    S = x.shape[1]
    topk = min(IDX_TOPK_MAX, S // 4)
    rope128 = rope_tables(S, HEAD_DIM)
    rope64 = rope_tables(S, IDX_DIM)
    for layer in range(DEPTH):
        j = layer // 2
        if layer % 2 == 0:
            x = even_layer(x, norm_even[j], w_in_even[j], b_f_even[j], g_qk_fox[j], g_qk_dsa[j],
                           g_kidx[j], w_out_even[j], rope128, rope64, topk)
        else:
            x = odd_layer(x, norm_odd[j], w_in_odd[j], g_qk_swa[j], sinks[j], w_out_odd[j], rope64)
    return x


_drawn_inputs = setup_inputs


def setup_inputs(seed=0):
    import zlib

    import numpy as np

    out = dict(_drawn_inputs(seed))
    spreads = {}
    factors = {'norm_even': 3.835,
     'b_f_even': 4.288,
     'g_qk_fox': 8.0,
     'g_qk_dsa': 8.0,
     'g_kidx': 6.165,
     'norm_odd': 8.0,
     'g_qk_swa': 8.0,
     'sinks': 33.726}
    for name, (base, spread) in spreads.items():
        noise = np.random.default_rng([zlib.crc32(name.encode()), seed]).standard_normal(out[name].shape)
        drawn = base * np.exp(spread * noise) if base else spread * noise
        out[name] = __import__('jax').numpy.asarray(drawn.astype(out[name].dtype))
    for name, factor in factors.items():
        out[name] = (out[name] * factor).astype(out[name].dtype)
    return out
```

```python
from contextlib import ExitStack

import concourse.bass as bass
from concourse import mybir

F32 = mybir.dt.float32
F32R = mybir.dt.float32r
ALU = mybir.AluOpType
ACT = mybir.ActivationFunctionType
AX = mybir.AxisListType

P = 128
T = 2
CW = 512
VK = 2
RAW = 4
HL = 4
EPS = 1e-6
MASKED = 1e30
TAKEN = -3e38

SCORES_AT = [1, 4, 7, 10]
FLIP_AT = [3, 6, 9, 12]
PV_AT = [4, 7, 10, 13]
YFLIP_AT = [6, 9, 12, 15]


class Steps:

    def __init__(self, eng, sem):
        self.eng, self.sem, self.n, self.base = eng, sem, 0, 0

    def did(self, instruction):
        instruction.then_inc(self.sem, 1)
        self.n += 1

    def settle(self):
        self.eng.wait_ge(self.sem, self.base + self.n)

    def enter(self, turn, per_turn):
        self.base, self.start, self.per = turn * per_turn, self.n, per_turn

    def leave(self, turns):
        assert self.n - self.start == self.per, (self.sem, self.n - self.start)
        self.n, self.base = self.start + self.per * turns, 0


def hybrid_trunk(nc, x, norm_even, w_in_even, b_f_even, g_qk_fox, g_qk_dsa, g_kidx, w_out_even,
                 norm_odd, w_in_odd, g_qk_swa, sinks, w_out_odd, rope, out):
    D = x.shape[2]
    KT = D // P
    OC = D // CW
    V = KT // VK
    EVEN = w_in_even.shape[2]
    H0, HD = 8, 128
    IH, ID = 16, 64
    SH, SKV, SD = 32, 4, 64
    TOPK = x.shape[1] // 4
    FW = H0 * HD
    AF = 4 * FW
    DSA = AF + H0
    IQ = DSA + 4 * FW
    IW = (EVEN - IQ) // 3
    IXW = IH * ID + ID + IH + H0
    IK, IWT, IAF = IH * ID, IH * ID + ID, IH * ID + ID + IH
    assert IW * 3 == EVEN - IQ and KT == 16 and OC == 4
    GROUP0 = 3
    OUT0 = GROUP0 + 16
    KV = OUT0 + OC
    SWA0 = KV + 1
    OUT1 = SWA0 + 8
    NCH = OUT1 + OC
    OUT_ORDER = ([(0, s) for s in range(6)] + [(1, s) for s in range(6)] + [(0, 6), (0, 7), (1, 6), (1, 7)]
                 + [(c, s) for c in (2, 3) for s in range(8)])

    ctx = ExitStack()
    with ctx:
        def sb(name, shape, dt=F32):
            return ctx.enter_context(nc.sbuf_tensor(name, shape, dt))

        def sem(name):
            return ctx.enter_context(nc.semaphore(name))

        x_hi, x_lo = sb("x_hi", [P, KT, T * P], F32R), sb("x_lo", [P, KT, T * P], F32R)
        y_hi, y_lo = sb("y_hi", [P, KT, T * P], F32R), sb("y_lo", [P, KT, T * P], F32R)
        w_raw = sb("w_raw", [P, RAW, VK, CW])
        w_hi, w_lo = sb("w_hi", [P, HL, VK, CW], F32R), sb("w_lo", [P, HL, VK, CW], F32R)
        resid = sb("resid", [P, T, D])
        ixT = sb("ixT", [P, 8, T * P])
        bias = sb("bias", [P, 12, 3 * P])
        tab_c, tab_s = sb("tab_c", [P, 6, T, HD]), sb("tab_s", [P, 6, T, HD])
        tab64_c, tab64_s = (t[:, 4:6, :, :].rearrange("p a t (b d) -> p (a t b d)", b=2)
                            .rearrange("p (k t d) -> p k t d", k=4, t=T) for t in (tab_c, tab_s))
        qk = sb("qk", [P, T, CW])
        sq = sb("sq", [P, T, CW])
        tmp = sb("tmp", [P, T, CW])
        vals = sb("vals", [P, T, CW])
        gate = sb("gate", [P, T, CW])
        qT, kT = sb("qT", [P, 4, T * P]), sb("kT", [P, 4, T * P])
        prob = sb("prob", [P, 2, 2, 3 * P])
        ysb = sb("ysb", [P, 2, T, P])
        kT_now, v_now = sb("kT_now", [P, T * P]), sb("v_now", [P, T, SD])
        ident = sb("ident", [P, P])
        mask = sb("mask", [P, 3 * P])
        norms = sb("norms", [P, 2 * KT])
        small = sb("small", [P, 360])
        col = iter(range(0, 360))

        def cols(n):
            a = [next(col) for _ in range(n)][0]
            return small[:, a:a + n]
        one_c = cols(1)
        ssq = cols(8).rearrange("p (t c) -> p t c", t=T)
        ssum = cols(T)
        var, lnv, r0, na, nb, rinv = (cols(16) for _ in range(6))
        rstd, nrstd = cols(T), cols(T)
        negmax = cols(8).rearrange("p (b a t) -> p b a t", b=2, a=2)
        rowmax = cols(8).rearrange("p (b a t) -> p b a t", b=2, a=2)
        rowsum = cols(8).rearrange("p (b a t) -> p b a t", b=2, a=2)
        esink = cols(8).rearrange("p (b a t) -> p b a t", b=2, a=2)
        rsum = cols(4).rearrange("p (a t) -> p a t", a=2)
        sink_now = cols(8)
        sinks_b = cols(SH)
        bf_b = cols(H0)
        zf, nzf, azf, mzf, ezf, lzf, logf = (cols(T * H0).rearrange("p (t h) -> p t h", t=T) for _ in range(7))
        cq = cols(T * H0).rearrange("p (t h) -> p t h", t=T)
        top8 = cols(8)
        ssumq = cols(16)
        spare = cols(1)
        tri = ysb[:, :, :, :].rearrange("p b t n -> p (b t n)")[:, 0:2 * P]
        norm_rows = qT[0:2 * KT, 0, 0:P]
        rope_sb = kT[:, :, :].rearrange("p h n -> p (h n)")[:, 0:T * (HD + SD)].rearrange("p (t n) -> p t n", t=T)
        probT = ixT[:, :, :].rearrange("p h n -> p (h n)")[:, 0:2 * 3 * P].rearrange("p (a n) -> p a n", a=2)
        ix = resid[:, :, :].rearrange("p t d -> p (t d)")[:, 0:T * IXW].rearrange("p (t n) -> p t n", t=T)
        score = resid[:, :, :].rearrange("p t d -> p (t d)")[:, T * IXW:T * IXW + 3 * P]
        ikn = resid[:, :, :].rearrange("p t d -> p (t d)")[:, T * IXW + 3 * P:T * IXW + 3 * P + 512].rearrange(
            "p (t a d) -> p t a d", t=T, a=4)
        ikT = kT_now
        gains = qk[:, :, :].rearrange("p t n -> p (t n)")
        lf_b = [vals[:, :, :].rearrange("p t (h n) -> p t h n", h=4), gate[:, :, :].rearrange("p t (h n) -> p t h n", h=4)]

        ps_proj = [ctx.enter_context(nc.psum_tensor(f"ps_proj{i}", [P, CW], F32)) for i in range(4)]
        ps_s = ctx.enter_context(nc.psum_tensor("ps_s", [P, CW], F32))
        ps_t = ctx.enter_context(nc.psum_tensor("ps_t", [P, CW], F32))
        ps_p = ctx.enter_context(nc.psum_tensor("ps_p", [P, CW], F32))
        ps_o = ctx.enter_context(nc.psum_tensor("ps_o", [P, CW], F32))

        x_landed = [sem(f"x_landed{c}") for c in range(4)]
        small_landed = sem("small_landed")
        resid_landed = sem("resid_landed")
        w_landed = [sem(f"w_landed{i}") for i in range(RAW)]
        out_stored = sem("out_stored")
        hi_ready, lo_ready, visit_done = sem("hi_ready"), sem("lo_ready"), sem("visit_done")
        chunk_read = sem("chunk_read")
        out_added = sem("out_added")
        consts_ready = sem("consts_ready")
        tables_ready = sem("tables_ready")
        norms_flipped, norms_ready = sem("norms_flipped"), sem("norms_ready")
        x_flipped, xhi_ready, xlo_ready = sem("x_flipped"), sem("xhi_ready"), sem("xlo_ready")
        squares_ready = sem("squares_ready")
        var_ready, root_ready = sem("var_ready"), sem("root_ready")
        rstd_ready = sem("rstd_ready")
        qk_read, qk_normed, qk_swapped, qk_ready = sem("qk_read"), sem("qk_normed"), sem("qk_swapped"), sem("qk_ready")
        qk_flipped, qkT_ready = sem("qk_flipped"), sem("qkT_ready")
        vals_ready, sig_ready, gate_ready = sem("vals_ready"), sem("sig_ready"), sem("gate_ready")
        scores_done, max_ready, prob_ready = sem("scores_done"), sem("max_ready"), sem("prob_ready")
        prob_flipped, probT_ready = sem("prob_flipped"), sem("probT_ready")
        pv_done, y_ready, y_flipped, yhi_ready, ylo_ready = (
            sem("pv_done"), sem("y_ready"), sem("y_flipped"), sem("yhi_ready"), sem("ylo_ready"))
        kv_picked, sinks_picked = sem("kv_picked"), sem("sinks_picked")
        ix_swapped, ix_roped, ix_flipped, ixT_ready = sem("ix_swapped"), sem("ix_roped"), sem("ix_flipped"), sem("ixT_ready")
        ik_swapped, ik_read = sem("ik_swapped"), sem("ik_read")
        logits_done, relu_ready, weighed = sem("logits_done"), sem("relu_ready"), sem("weighed")
        gate_abs, gate_soft, logf_ready, lfb_ready = sem("gate_abs"), sem("gate_soft"), sem("logf_ready"), sem("lfb_ready")
        cq_done, cq_ready, ck_done, ck_read = sem("cq_done"), sem("cq_ready"), sem("ck_done"), sem("ck_read")
        dve_did, act_did, pool_did = sem("dve_did"), sem("act_did"), sem("pool_did")

        w0 = w_in_even[0].rearrange("(k p) n -> p k n", p=P)
        w1 = w_in_odd[0].rearrange("(k p) n -> p k n", p=P)
        wo0 = w_out_even[0].rearrange("(k p) n -> p k n", p=P)
        wo1 = w_out_odd[0].rearrange("(k p) n -> p k n", p=P)
        x_dram = x[0].rearrange("(t p) d -> p t d", p=P)
        out_dram = out[0].rearrange("(t p) d -> p t d", p=P)
        rope_dram = rope.rearrange("(t p) d -> p t d", p=P)
        N_SMALL = 16 * 9

        def chunk_width(c):
            return (IW, IW, IW + H0)[c] if isinstance(c, int) and c < GROUP0 else CW

        def landed_count(c, s):
            turns = 2 * c + s // RAW
            if isinstance(c, int) and c < GROUP0:
                return 16 * (turns + 1) + (16 * (turns - 3) if c == 2 else 0)
            return 16 * (turns + 1) + 32

        def event_of(kind, k=0):
            return {"rstd0": 0, "ik": 1, "even": 2 + k, "rstd1": 10, "kv": 11, "odd": 12 + k}[kind]

        block = ctx.enter_context(nc.Block())

        @block.sync
        def _(sp):
            for c in range(OC):
                sp.dma_start(resid[:, :, c * CW:(c + 1) * CW], x_dram[:, :, c * CW:(c + 1) * CW]).then_inc(x_landed[c], 16)

            def weights(c, s, src, first_col, width=CW, at=0, k_tile=None):
                k = VK * s if k_tile is None else k_tile
                return sp.dma_start(w_raw[:, s % RAW, :, at:at + width],
                                    src[:, k:k + VK, bass.ds(first_col, width)]).then_inc(w_landed[s % RAW], 16)

            def ring_free(c, s):
                if not isinstance(c, int) or V * c + s >= RAW:
                    sp.wait_ge(lo_ready, V * c + s - RAW + 1)

            for c in range(GROUP0):
                for s in range(V):
                    ring_free(c, s)
                    weights(c, s, w0, IQ + IW * c, IW)
                    if c == GROUP0 - 1:
                        weights(c, s, w0, AF, H0, at=IW)
            with sp.Fori(0, 2) as kind:
                with sp.Fori(0, 2) as half:
                    with sp.Fori(0, 4) as part:
                        for s in range(V):
                            c = kind * 8 + half * 4 + part + GROUP0
                            ring_free(c, s)
                            weights(c, s, w0, kind * DSA + half * CW + part * FW)
            sp.wait_ge(weighed, 9 + 9)
            for c in range(OC):
                sp.dma_start(resid[:, :, c * CW:(c + 1) * CW], x_dram[:, :, c * CW:(c + 1) * CW]).then_inc(resid_landed, 16)
            for v, (c, s) in enumerate(OUT_ORDER):
                ring_free(OUT0 + v // V, v % V)
                weights(OUT0, v % V, wo0, c * CW, k_tile=VK * s)
            for s in range(V):
                ring_free(KV, s)
                weights(KV, s, w1, SH * SD)
            with sp.Fori(0, 4) as group:
                for part in range(2):
                    for s in range(V):
                        c = group * 2 + part + SWA0
                        ring_free(c, s)
                        weights(c, s, w1, group * CW + part * (SH * SD + 2 * SKV * SD))
            for v, (c, s) in enumerate(OUT_ORDER):
                ring_free(OUT1 + v // V, v % V)
                weights(OUT1, v % V, wo1, c * CW, k_tile=VK * s)
            for c in range(OC):
                sp.wait_ge(out_added, OC + c + 1)
                sp.dma_start(out_dram[:, :, c * CW:(c + 1) * CW], resid[:, :, c * CW:(c + 1) * CW]).then_inc(out_stored, 16)
            sp.wait_ge(out_stored, 16 * OC)

        @block.tensor
        def _(pe):
            def project(c, s, bank, acts_hi, acts_lo, kt=None, width=CW, first=False, last=False):
                k0 = VK * s if kt is None else kt
                pe.wait_ge(lo_ready, V * c + s + 1)
                for k in range(VK):
                    for t in range(T):
                        o = ps_proj[2 * bank + t][:, 0:width]
                        a_hi = acts_hi[:, k0 + k, t * P:(t + 1) * P]
                        a_lo = acts_lo[:, k0 + k, t * P:(t + 1) * P]
                        h, l = w_hi[:, s % HL, k, 0:width], w_lo[:, s % HL, k, 0:width]
                        nc.tensor.matmul(o, a_hi, h, start=first and k == 0, stop=False)
                        nc.tensor.matmul(o, a_hi, l, start=False, stop=False)
                        mm = nc.tensor.matmul(o, a_lo, h, start=False, stop=last and k == VK - 1)
                mm.then_inc(visit_done, 1)

            def chunk_visit(c, s, bank, layer, width=CW):
                if s == 0:
                    if not isinstance(c, int) or c >= 2:
                        act_chunks = c - 1 if layer == 0 else c - 1 - OC
                        if isinstance(c, int) and c in (KV, SWA0):
                            pe.wait_ge(out_added, c - KV + OC - 1)
                        else:
                            pe.wait_ge(chunk_read, act_chunks)
                if isinstance(c, int) and (c in (0, KV)) and s % 2 == 0:
                    pe.wait_ge(xlo_ready, OC * layer + s // 2 + 1)
                project(c, s, bank, x_hi, x_lo, width=width, first=s == 0, last=s == V - 1)

            def flip_x(layer, c):
                banks = (ps_s, ps_t) if c % 2 == 0 else (ps_p, ps_o)
                if layer == 0:
                    pe.wait_ge(x_landed[c], 16)
                else:
                    pe.wait_ge(out_added, c + 1)
                if c >= 2:
                    pe.wait_ge(xlo_ready, OC * layer + c - 1)
                for k in range(4):
                    for t in range(T):
                        a = (k % 2) * 2 * P + t * P
                        mm = nc.tensor.transpose(banks[k // 2][:, a:a + P],
                                                 resid[:, t, c * CW + k * P:c * CW + (k + 1) * P], ident[:, :])
                mm.then_inc(x_flipped, 1)

            def flip_qk(step, half):
                pe.wait_ge(qk_ready, step // 2 + 1)
                if not isinstance(step, int) or step >= 1:
                    pe.wait_ge(qkT_ready, step)
                for b in range(2):
                    for t in range(T):
                        a = b * 2 * P + t * P
                        mm = nc.tensor.transpose(ps_t[:, a:a + P], qk[:, t, (2 * half + b) * P:(2 * half + b + 1) * P],
                                                 ident[:, :])
                mm.then_inc(qk_flipped, 1)

            def scores_even(n, j, group):
                if j == 0:
                    pe.wait_ge(qkT_ready, 4 * (group + 1))
                nc.tensor.matmul(ps_s[:, 0:P], qT[:, j, 0:P], kT[:, j, 0:P], start=True, stop=True)
                nc.tensor.matmul(ps_s[:, P:3 * P], qT[:, j, P:2 * P], kT[:, j, :], start=True, stop=True)\
                    .then_inc(scores_done, 1)

            def scores_odd(n, j, group):
                if j == 0:
                    pe.wait_ge(qkT_ready, 16 + 2 + 2 * (group + 1))
                    pe.wait_ge(kv_picked, 2 * (group + 1))
                for a, bank in enumerate((ps_s, ps_t)):
                    r = slice(a * SD, (a + 1) * SD)
                    nc.tensor.matmul(bank[:, 0:P], qT[r, j, 0:P], kT_now[r, 0:P], start=True, stop=True)
                    mm = nc.tensor.matmul(bank[:, P:3 * P], qT[r, j, P:2 * P], kT_now[r, :], start=True, stop=True)
                mm.then_inc(scores_done, 1)

            def flip_prob(n, j, odd):
                pe.wait_ge(prob_ready, n + 1)
                for a in range(2 if odd else 1):
                    bank = (ps_p, ps_s)[a]
                    for b in range(3):
                        mm = nc.tensor.transpose(bank[:, b * P:(b + 1) * P], prob[:, j % 2, a, b * P:(b + 1) * P],
                                                 ident[:, :])
                mm.then_inc(prob_flipped, 1)

            def pv_even(n, j, group):
                pe.wait_ge(probT_ready, n + 1)
                if j == 0:
                    pe.wait_ge(vals_ready, group + 1)
                else:
                    pe.wait_ge(ylo_ready, n)
                v = [vals[:, t, j * P:(j + 1) * P] for t in range(T)]
                nc.tensor.matmul(ps_o[:, 0:P], probT[:, 0, 0:P], v[0], start=True, stop=True)
                nc.tensor.matmul(ps_o[:, P:2 * P], probT[:, 0, P:2 * P], v[0], start=True, stop=False)
                nc.tensor.matmul(ps_o[:, P:2 * P], probT[:, 0, 2 * P:3 * P], v[1], start=False, stop=True)\
                    .then_inc(pv_done, 1)

            def pv_odd(n, j, group):
                pe.wait_ge(probT_ready, n + 1)
                if j:
                    pe.wait_ge(ylo_ready, n)
                for a in range(2):
                    o = [ps_o[:, t * P + a * SD:t * P + (a + 1) * SD] for t in range(T)]
                    nc.tensor.matmul(o[0], probT[:, a, 0:P], v_now[:, 0, :], start=True, stop=True)
                    nc.tensor.matmul(o[1], probT[:, a, P:2 * P], v_now[:, 0, :], start=True, stop=False)
                    mm = nc.tensor.matmul(o[1], probT[:, a, 2 * P:3 * P], v_now[:, 1, :], start=False, stop=True)
                mm.then_inc(pv_done, 1)

            def flip_y(n, j):
                pe.wait_ge(y_ready, n + 1)
                for t in range(T):
                    mm = nc.tensor.transpose(ps_o[:, 2 * P + t * P:2 * P + (t + 1) * P], ysb[:, j % 2, t, :], ident[:, :])
                mm.then_inc(y_flipped, 1)

            def attention(h, base, group, odd):
                for j in range(4):
                    if h == YFLIP_AT[j]:
                        flip_y(base + j, j)
                for j in range(4):
                    if h == PV_AT[j]:
                        (pv_odd if odd else pv_even)(base + j, j, group)
                for j in range(4):
                    if h == FLIP_AT[j]:
                        flip_prob(base + j, j, odd)
                for j in range(4):
                    if h == SCORES_AT[j]:
                        (scores_odd if odd else scores_even)(base + j, j, group)

            def output_stage(layer):
                c0 = OUT1 if layer else OUT0
                base = 16 * layer + 12
                for v, (c, s) in enumerate(OUT_ORDER):
                    if v < 12 and v % 6 == 0:
                        if layer == 0 or c < 2:
                            pe.wait_ge(chunk_read, (19 if layer == 0 else 28) - 1 + c)
                    if s == 0 and c >= 2:
                        pe.wait_ge(out_added, OC * layer + c - 1)
                    if v == 0:
                        pe.wait_ge(ylo_ready, base)
                    if v == 12:
                        for h in range(12, 16):
                            attention(h, base, 3, layer == 1)
                        pe.wait_ge(ylo_ready, base + 4)
                    if layer == 0 and v == 20:
                        flip_x(1, 0)
                    if layer == 0 and v == 23:
                        flip_x(1, 1)
                    if layer == 0 and v == 29:
                        flip_x(1, 2)
                    project(c0 + v // V, v % V, (c0 + c) % 2, y_hi, y_lo, kt=VK * s, first=s == 0, last=s == 7)
                    if v < 12:
                        attention(v, base, 3, layer == 1)

            pe.wait_ge(consts_ready, 1)
            pe.wait_ge(small_landed, N_SMALL)
            nc.tensor.transpose(ps_proj[3][:, 0:2 * KT], norm_rows, ident[0:2 * KT, 0:2 * KT]).then_inc(norms_flipped, 1)
            for c in range(OC):
                flip_x(0, c)
            for c in range(GROUP0):
                for s in range(V):
                    if c == 1 and s == 0:
                        pe.wait_ge(norms_ready, 1)
                    chunk_visit(c, s, c % 2, 0, chunk_width(c))

            pe.wait_ge(consts_ready, 2)
            for part in range(4):
                for s in range(V):
                    h = V * part + s
                    chunk_visit(GROUP0 + part, s, (GROUP0 + part) % 2, 0)
                    if h == 3:
                        pe.wait_ge(logf_ready, 1)
                        nc.tensor.matmul(ps_o[:, 0:H0], tri[:, 0:P], logf[:, 0, :], start=True, stop=True)
                        nc.tensor.matmul(ps_o[:, H0:2 * H0], tri[:, P:2 * P], logf[:, 0, :], start=True, stop=False)
                        nc.tensor.matmul(ps_o[:, H0:2 * H0], tri[:, 0:P], logf[:, 1, :], start=False, stop=True)\
                            .then_inc(cq_done, 1)
                    if 5 <= h < 9:
                        i = h - 5
                        pe.wait_ge(ix_roped, 3)
                        if i == 3:
                            pe.wait_ge(cq_ready, 1)
                        bank = (ps_s, ps_t, ps_p, ps_o)[i]
                        for b in range(2):
                            for t in range(T):
                                a = b * 2 * P + t * P
                                mm = nc.tensor.transpose(bank[:, a:a + P], ix[:, t, (2 * i + b) * P:(2 * i + b + 1) * P],
                                                         ident[:, :])
                        mm.then_inc(ix_flipped, 1)
                    if h == 9:
                        pe.wait_ge(ixT_ready, 2)
                        for t in range(T):
                            mm = nc.tensor.transpose(ps_t[:, t * P:(t + 1) * P],
                                                     ikn[:, t, 2:4, :].rearrange("p a d -> p (a d)"), ident[:, :])
                        mm.then_inc(ix_flipped, 1)
                    if 10 <= h < 14:
                        i = h - 10
                        pe.wait_ge(lfb_ready, 1)
                        pe.wait_ge(ixT_ready, 4)
                        if i >= 1:
                            pe.wait_ge(ck_read, i)
                        for b in range(2):
                            hh = 2 * i + b
                            lf = lf_b[hh // 4]
                            o = ps_o[:, b * 2 * P:(b + 1) * 2 * P]
                            nc.tensor.matmul(o, lf[:, 0, hh % 4, :], tri, start=True, stop=False)
                            mm = nc.tensor.matmul(o[:, P:2 * P], lf[:, 1, hh % 4, :], tri[:, 0:P], start=False, stop=True)
                        mm.then_inc(ck_done, 1)
                    if 11 <= h < 19:
                        i = h - 11
                        pe.wait_ge(ixT_ready, 5)
                        if i >= 1:
                            pe.wait_ge(relu_ready, i)
                        for a, bank in enumerate((ps_s, ps_p)):
                            r = slice(a * ID, (a + 1) * ID)
                            nc.tensor.matmul(bank[:, 0:P], ixT[r, i, 0:P], ikT[r, 0:P], start=True, stop=True)
                            mm = nc.tensor.matmul(bank[:, P:3 * P], ixT[r, i, P:2 * P], ikT[r, :], start=True, stop=True)
                        mm.then_inc(logits_done, 1)
                    if h in (14, 15):
                        flip_qk(h - 14, h - 14)
                    if h in (22, 23):
                        flip_qk(h - 20, h - 22)
            pe.wait_ge(relu_ready, 8)
            pe.wait_ge(ck_read, 4)
            with pe.Fori(0, 3) as turn:
                for part in range(4):
                    for s in range(V):
                        h = V * part + s
                        chunk_visit(turn * 4 + part + GROUP0 + 4, s, (GROUP0 + part) % 2, 0)
                        attention(h, turn * 4, turn, False)
                        if h in (14, 15):
                            flip_qk(turn * 4 + 4 + h - 14, h - 14)
                        if h in (22, 23):
                            flip_qk(turn * 4 + 6 + h - 22, h - 22)
            output_stage(0)

            for s in range(V):
                if s == 5:
                    flip_x(1, 3)
                chunk_visit(KV, s, KV % 2, 1)
            for part in range(2):
                for s in range(V):
                    h = V * part + s
                    chunk_visit(SWA0 + part, s, part, 1)
                    if h in (5, 6):
                        flip_qk(16 + h - 5, h - 5)
                    if h in (13, 15):
                        flip_qk(18 + (h - 13) // 2, (h - 13) // 2)
            with pe.Fori(0, 3) as turn:
                for part in range(2):
                    for s in range(V):
                        h = V * part + s
                        chunk_visit(turn * 2 + part + SWA0 + 2, s, part, 1)
                        attention(h, turn * 4 + 16, turn, True)
                        if h in (14, 15):
                            flip_qk(turn * 2 + 20 + h - 14, h - 14)
            output_stage(1)

        @block.scalar
        def _(act):
            own = Steps(act, act_did)

            def split_hi(c, s, width=CW):
                act.wait_ge(w_landed[s % RAW], landed_count(c, s))
                if not isinstance(c, int) or V * c + s >= HL:
                    act.wait_ge(visit_done, V * c + s - HL + 1)
                nc.scalar.activation(w_hi[:, s % HL, :, 0:width], w_raw[:, s % RAW, :, 0:width], ACT.Copy)\
                    .then_inc(hi_ready, 1)

            def ahead(c, s, next_width=CW):
                if s < V - 2:
                    split_hi(c, s + 2, chunk_width(c))
                else:
                    split_hi(c + 1, s + 2 - V, next_width)

            def x_hi_part(layer, c):
                banks = (ps_s, ps_t) if c % 2 == 0 else (ps_p, ps_o)
                if layer == 0:
                    act.wait_ge(x_landed[c], 16)
                else:
                    act.wait_ge(out_added, c + 1)
                if OC * layer + c:
                    act.wait_ge(squares_ready, OC * layer + c)
                for t in range(T):
                    i = nc.scalar.activation(tmp[:, t, :], resid[:, t, c * CW:(c + 1) * CW], ACT.Square,
                                             accum_out=ssq[:, t, c:c + 1])
                i.then_inc(squares_ready, 1)
                act.wait_ge(x_flipped, OC * layer + c + 1)
                for k in range(4):
                    kt = 4 * c + k
                    i = nc.scalar.activation(x_hi[:, kt, :], banks[k // 2][:, (k % 2) * 2 * P:(k % 2 + 1) * 2 * P],
                                             ACT.Copy, scale=norms[:, KT * layer + kt:KT * layer + kt + 1])
                i.then_inc(xhi_ready, 1)

            def root(e, n):
                act.wait_ge(var_ready, e + 1)
                own.did(nc.scalar.activation(lnv[:, 0:n], var[:, 0:n], ACT.Ln))
                own.settle()
                nc.scalar.activation(r0[:, 0:n], lnv[:, 0:n], ACT.Exp, scale=-0.5).then_inc(root_ready, 1)

            def read_index(c):
                act.wait_ge(visit_done, V * (c + 1))
                if c == 0:
                    act.wait_ge(rstd_ready, 1)
                width = chunk_width(c)
                for t in range(T):
                    i = nc.scalar.activation(ix[:, t, IW * c:IW * c + width], ps_proj[2 * (c % 2) + t][:, 0:width],
                                             ACT.Copy, scale=rstd[:, t:t + 1])
                i.then_inc(chunk_read, 1)

            def read_qk(c, bank, width, k, settled):
                act.wait_ge(visit_done, (c + 1) * V)
                if not isinstance(k, int) or k >= 1:
                    act.wait_ge(qk_flipped, 2 * k)
                if settled is not None:
                    act.wait_ge(gate_ready, settled)
                for t in range(T):
                    ps = ps_proj[2 * bank + t][:, 0:width]
                    if width == CW:
                        q_to, s_to = qk[:, t, :], sq[:, t, :]
                    else:
                        q_to, s_to = (b[:, :, :].rearrange("p t n -> p (t n)")[:, t * width:(t + 1) * width] for b in (qk, sq))
                    nc.scalar.activation(q_to, ps, ACT.Copy, scale=rstd[:, t:t + 1])
                    i = nc.scalar.activation(s_to, ps, ACT.Square, scale=rstd[:, t:t + 1])
                i.then_inc(qk_read, 1)

            def copy_marker(to):
                own_i = nc.scalar.activation(lnv[:, 15:16], one_c, ACT.Copy)
                own_i.then_inc(to, 1)

            def read_vals(c, bank, at=0, width=CW):
                act.wait_ge(visit_done, (c + 1) * V)
                for t in range(T):
                    i = nc.scalar.activation(vals[:, t, 0:width], ps_proj[2 * bank + t][:, at:at + width],
                                             ACT.Copy, scale=rstd[:, t:t + 1])
                i.then_inc(vals_ready, 1)

            def read_gate(c, bank):
                act.wait_ge(visit_done, (c + 1) * V)
                for t in range(T):
                    ps = ps_proj[2 * bank + t][:, :]
                    nc.scalar.activation(gate[:, t, :], ps, ACT.Copy, scale=rstd[:, t:t + 1])
                    i = nc.scalar.activation(sq[:, t, :], ps, ACT.Exp, scale=nrstd[:, t:t + 1])
                    own.did(i)
                own.settle()
                own.did(nc.scalar.activation(sq[:, :, :], sq[:, :, :], ACT.Ln, bias=one_c))
                own.settle()
                nc.scalar.activation(sq[:, :, :], sq[:, :, :], ACT.Exp, scale=-1.0).then_inc(sig_ready, 1)

            def move_qkT(step, half, to):
                act.wait_ge(qk_flipped, step + 1)
                nc.scalar.activation(to[:, 2 * half:2 * half + 2, :].rearrange("p b n -> p (b n)"), ps_t[:, :], ACT.Copy)\
                    .then_inc(qkT_ready, 1)

            def exp_scores(n, j, odd):
                act.wait_ge(max_ready, n + 1)
                for a in range(2 if odd else 1):
                    for t in range(T):
                        r = (slice(0, P), slice(P, 3 * P))[t]
                        if odd:
                            nc.scalar.activation(esink[:, j % 2, a, t:t + 1], sink_now[:, 2 * j + a:2 * j + a + 1], ACT.Exp,
                                                 bias=negmax[:, j % 2, a, t:t + 1])
                        i = nc.scalar.activation(prob[:, j % 2, a, r], prob[:, j % 2, a, r], ACT.Exp,
                                                 bias=negmax[:, j % 2, a, t:t + 1], accum_out=rowsum[:, j % 2, a, t:t + 1])
                i.then_inc(prob_ready, 1)

            def move_probT(n, j, odd):
                act.wait_ge(prob_flipped, n + 1)
                for a in range(2 if odd else 1):
                    i = nc.scalar.activation(probT[:, a, :], (ps_p, ps_s)[a][:, 0:3 * P], ACT.Copy)
                i.then_inc(probT_ready, 1)

            def y_hi_part(n, kt):
                act.wait_ge(y_flipped, n + 1)
                nc.scalar.activation(y_hi[:, kt, :], ps_o[:, 2 * P:4 * P], ACT.Copy).then_inc(yhi_ready, 1)

            def attention(h, base, kt, odd):
                for j in range(4):
                    if h == YFLIP_AT[j]:
                        y_hi_part(base + j, kt + j)
                for j in range(4):
                    if h == FLIP_AT[j]:
                        move_probT(base + j, j, odd)
                for j in range(4):
                    if h == SCORES_AT[j]:
                        exp_scores(base + j, j, odd)

            def output_stage(layer):
                c0 = OUT1 if layer else OUT0
                for v in range(len(OUT_ORDER)):
                    if not (layer and v >= len(OUT_ORDER) - 2):
                        ahead(c0 + v // V, v % V)
                    if v == 0:
                        read_gate(c0 - 1, (c0 - 1) % 2)
                        copy_marker(chunk_read)
                    if layer and v == 1:
                        act.wait_ge(sinks_picked, 4)
                    for h in ((v,) if v < 12 else (12, 13) if v == 12 else (14, 15) if v == 13 else ()):
                        attention(h, 16 * layer + 12, 12, layer == 1)
                    if layer == 0:
                        for c, at in enumerate((20, 23, 29)):
                            if v == at:
                                x_hi_part(1, c)

            flat = qk[:, :, :].rearrange("p t n -> p (t n)")
            for to, src in ((qT[0:KT, 0, 0:P], norm_even[0].rearrange("(k p) -> k p", p=P)),
                            (qT[KT:2 * KT, 0, 0:P], norm_odd[0].rearrange("(k p) -> k p", p=P)),
                            (rope_sb, rope_dram),
                            (flat[:, 0:2 * HD], g_qk_fox.rearrange("a b d -> a (b d)")[0].partition_broadcast(P)),
                            (flat[:, 2 * HD:4 * HD], g_qk_dsa.rearrange("a b d -> a (b d)")[0].partition_broadcast(P)),
                            (flat[:, 4 * HD:4 * HD + ID], g_kidx[0].partition_broadcast(P)),
                            (flat[:, 4 * HD + ID:4 * HD + ID + 2 * SD],
                             g_qk_swa.rearrange("a b d -> a (b d)")[0].partition_broadcast(P)),
                            (sinks_b, sinks[0].partition_broadcast(P)),
                            (bf_b, b_f_even[0].partition_broadcast(P))):
                act.dma_start(to, src).then_inc(small_landed, 16)
            act.wait_ge(consts_ready, 2)
            act.wait_ge(norms_flipped, 1)
            nc.scalar.activation(norms[:, :], ps_proj[3][:, 0:2 * KT], ACT.Copy).then_inc(norms_ready, 1)
            act.wait_ge(norms_ready, 1)
            for s in range(2):
                split_hi(0, s, IW)
            for c in range(OC):
                x_hi_part(0, c)
            root(event_of("rstd0"), T)
            for c in range(GROUP0):
                for s in range(V):
                    ahead(c, s, chunk_width(c + 1))
                    if c >= 1 and s == 0:
                        read_index(c - 1)

            for part in range(4):
                for s in range(V):
                    h = V * part + s
                    ahead(GROUP0 + part, s)
                    if h == 0:
                        read_index(2)
                        root(event_of("ik"), T)
                        act.wait_ge(gate_abs, 1)
                        own.did(nc.scalar.activation(ezf, azf, ACT.Exp, scale=-1.0))
                        own.settle()
                        nc.scalar.activation(lzf, ezf, ACT.Ln, bias=one_c).then_inc(gate_soft, 1)
                    if 5 <= h < 9:
                        act.wait_ge(ix_flipped, h - 4)
                        nc.scalar.activation(ixT[:, 2 * (h - 5):2 * (h - 5) + 2, :].rearrange("p b n -> p (b n)"),
                                             (ps_s, ps_t, ps_p, ps_o)[h - 5][:, :], ACT.Copy).then_inc(ixT_ready, 1)
                    if h == 9:
                        act.wait_ge(ix_flipped, 5)
                        nc.scalar.activation(ikT[:, :], ps_t[:, 0:2 * P], ACT.Copy).then_inc(ixT_ready, 1)
                    if h == V:
                        read_qk(GROUP0, GROUP0 % 2, CW, 0, None)
                        copy_marker(chunk_read)
                    if h == V + 2:
                        root(event_of("even", 0), 8)
                    if 11 <= h < 19:
                        i = h - 11
                        act.wait_ge(logits_done, i + 1)
                        if i >= 2:
                            act.wait_ge(weighed, i - 1)
                        for a, bank in enumerate((ps_s, ps_p)):
                            r = nc.scalar.activation(prob[:, i % 2, a, :], bank[:, 0:3 * P], ACT.Relu, scale=ID ** -0.5)
                        r.then_inc(relu_ready, 1)
                    if h in (14, 15):
                        move_qkT(h - 14, h - 14, qT)
                    if h == 2 * V:
                        read_qk(GROUP0 + 1, (GROUP0 + 1) % 2, CW, 1, None)
                        copy_marker(chunk_read)
                    if h == 2 * V + 2:
                        root(event_of("even", 1), 8)
                    if h in (22, 23):
                        move_qkT(h - 20, h - 22, kT)
                    if h == 3 * V:
                        read_vals(GROUP0 + 2, (GROUP0 + 2) % 2)
                        copy_marker(chunk_read)
            with act.Fori(0, 3) as turn:
                own.enter(turn, 5)
                c0 = turn * 4 + GROUP0 + 4
                for part in range(4):
                    for s in range(V):
                        h = V * part + s
                        ahead(c0 + part, s)
                        if h == 0:
                            read_gate(c0 - 1, (GROUP0 + 3) % 2)
                            copy_marker(chunk_read)
                        attention(h, turn * 4, turn * 4, False)
                        if h == V:
                            read_qk(c0, GROUP0 % 2, CW, turn * 2 + 2, turn + 1)
                            copy_marker(chunk_read)
                        if h == V + 2:
                            root(turn * 2 + event_of("even", 2), 8)
                        if h in (14, 15):
                            move_qkT(turn * 4 + 4 + h - 14, h - 14, qT)
                        if h == 2 * V:
                            read_qk(c0 + 1, (GROUP0 + 1) % 2, CW, turn * 2 + 3, None)
                            copy_marker(chunk_read)
                        if h == 2 * V + 2:
                            root(turn * 2 + event_of("even", 3), 8)
                        if h in (22, 23):
                            move_qkT(turn * 4 + 6 + h - 22, h - 22, kT)
                        if h == 3 * V:
                            read_vals(c0 + 2, (GROUP0 + 2) % 2)
                            copy_marker(chunk_read)
                own.leave(3)
            output_stage(0)

            for s in range(V):
                ahead(KV, s)
                if s == 5:
                    x_hi_part(1, 3)
                    root(event_of("rstd1"), T)
            for part in range(2):
                for s in range(V):
                    h = V * part + s
                    ahead(SWA0 + part, s)
                    if h == 0:
                        act.wait_ge(rstd_ready, 2)
                        read_qk(KV, KV % 2, SKV * SD, 8, 4)
                        read_vals(KV, KV % 2, SKV * SD, SKV * SD)
                        copy_marker(chunk_read)
                    if h == 2:
                        root(event_of("kv"), 8)
                    if h in (5, 6):
                        move_qkT(16 + h - 5, h - 5, kT)
                    if h == V:
                        read_qk(SWA0, 0, CW, 9, None)
                        copy_marker(chunk_read)
                    if h == V + 2:
                        root(event_of("odd", 0), 16)
                    if h in (13, 15):
                        move_qkT(18 + (h - 13) // 2, (h - 13) // 2, qT)
            with act.Fori(0, 3) as turn:
                own.enter(turn, 4)
                c0 = turn * 2 + SWA0 + 2
                for part in range(2):
                    for s in range(V):
                        h = V * part + s
                        ahead(c0 + part, s)
                        if h == 0:
                            read_gate(c0 - 1, 1)
                            copy_marker(chunk_read)
                        if h == 1:
                            act.wait_ge(sinks_picked, turn + 1)
                        attention(h, turn * 4 + 16, turn * 4, True)
                        if h == V:
                            read_qk(c0, 0, CW, turn + 10, turn + 5)
                            copy_marker(chunk_read)
                        if h == V + 2:
                            root(turn + event_of("odd", 1), 16)
                        if h in (14, 15):
                            move_qkT(turn * 2 + 20 + h - 14, h - 14, qT)
                own.leave(3)
            output_stage(1)

        @block.vector
        def _(dve):
            own = Steps(dve, dve_did)
            v_ = nc.vector

            def split_lo(c, s, width=CW):
                dve.wait_ge(hi_ready, V * c + s + 1)
                v_.tensor_tensor(w_lo[:, s % HL, :, 0:width], w_raw[:, s % RAW, :, 0:width],
                                 w_hi[:, s % HL, :, 0:width], ALU.subtract).then_inc(lo_ready, 1)

            def ahead(c, s, next_width=CW):
                if s < V - 2:
                    split_lo(c, s + 2, chunk_width(c))
                else:
                    split_lo(c + 1, s + 2 - V, next_width)

            def x_lo_part(layer, c):
                banks = (ps_s, ps_t) if c % 2 == 0 else (ps_p, ps_o)
                dve.wait_ge(xhi_ready, OC * layer + c + 1)
                for k in range(4):
                    kt = 4 * c + k
                    i = v_.scalar_tensor_tensor(out=x_lo[:, kt, :], in0=banks[k // 2][:, (k % 2) * 2 * P:(k % 2 + 1) * 2 * P],
                                                scalar=norms[:, KT * layer + kt:KT * layer + kt + 1],
                                                in1=x_hi[:, kt, :], op0=ALU.mult, op1=ALU.subtract)
                i.then_inc(xlo_ready, 1)

            def variance(ss, n, count):
                own.settle()
                v_.tensor_scalar(var[:, 0:n], ss, 1.0 / count, EPS, ALU.mult, ALU.add).then_inc(var_ready, 1)

            def refine(e, n, to):
                dve.wait_ge(var_ready, e + 1)
                dve.wait_ge(root_ready, e + 1)
                own.did(v_.tensor_tensor(na[:, 0:n], r0[:, 0:n], r0[:, 0:n], ALU.mult))
                own.settle()
                own.did(v_.tensor_tensor(nb[:, 0:n], na[:, 0:n], var[:, 0:n], ALU.mult))
                own.settle()
                own.did(v_.tensor_scalar(na[:, 0:n], nb[:, 0:n], -0.5, 1.5, ALU.mult, ALU.add))
                own.settle()
                own.did(v_.tensor_tensor(to, na[:, 0:n], r0[:, 0:n], ALU.mult))
                own.settle()

            def stream_rstd(layer):
                dve.wait_ge(squares_ready, OC * (layer + 1))
                own.did(v_.tensor_reduce(ssum, ssq, AX.X, ALU.add))
                variance(ssum, T, D)
                refine(event_of(f"rstd{layer}"), T, rstd)
                v_.tensor_scalar(nrstd, rstd, -1.0, None, ALU.mult).then_inc(rstd_ready, 1)

            def heads(buf, nh, dh):
                return buf[:, :, :].rearrange("p t n -> p (t n)")[:, 0:T * nh * dh].rearrange("p (h d) -> p h d", d=dh)

            def per_tile(buf, nh, dh):
                return buf[:, :, :].rearrange("p t n -> p (t n)")[:, 0:T * nh * dh].rearrange("p (t h d) -> p t h d", t=T, d=dh)

            def qk_variance(k, nh, dh):
                dve.wait_ge(qk_read, k + 1)
                own.did(v_.tensor_reduce(ssumq[:, 0:T * nh], heads(sq, nh, dh), AX.X, ALU.add))
                variance(ssumq[:, 0:T * nh], T * nh, dh)

            def qk_norm(e, nh, dh):
                n = T * nh
                refine(e, n, rinv[:, 0:n])
                h = heads(qk, nh, dh)
                v_.tensor_tensor(h, h, rinv[:, 0:n].unsqueeze(2).to_broadcast([P, n, dh]), ALU.mult).then_inc(qk_normed, 1)

            def qk_cos(k, nh, dh, table):
                dve.wait_ge(qk_normed, k + 1)
                own.did(v_.tensor_tensor(per_tile(tmp, nh, dh), per_tile(qk, nh, dh),
                                         table.unsqueeze(2).to_broadcast([P, T, nh, dh]), ALU.mult))

            def qk_rope(k, nh, dh, twice=False):
                dve.wait_ge(qk_swapped, k + 1)
                own.settle()
                if twice:
                    to = qk[:, :, :].rearrange("p t (h a d) -> p t h a d", a=2, d=dh)
                    own.did(v_.tensor_tensor(to[:, :, :, 0, :], per_tile(tmp, nh, dh), per_tile(sq, nh, dh), ALU.add))
                    v_.tensor_tensor(to[:, :, :, 1, :], per_tile(tmp, nh, dh), per_tile(sq, nh, dh), ALU.add)\
                        .then_inc(qk_ready, 1)
                else:
                    v_.tensor_tensor(heads(qk, nh, dh), heads(tmp, nh, dh), heads(sq, nh, dh), ALU.add).then_inc(qk_ready, 1)

            def make_gate(k):
                dve.wait_ge(sig_ready, k + 1)
                v_.tensor_tensor(gate[:, :, :], gate[:, :, :], sq[:, :, :], ALU.mult).then_inc(gate_ready, 1)
                dve.wait_ge(gate_ready, k + 1)

            def shift_scores_even(n, j, slot):
                dve.wait_ge(scores_done, n + 1)
                own.did(v_.tensor_tensor(prob[:, j % 2, 0, :], ps_s[:, 0:3 * P], bias[:, slot, :], ALU.subtract))
                own.settle()
                v_.tensor_reduce(negmax[:, j % 2, 0, 0:1], prob[:, j % 2, 0, 0:P], AX.X, ALU.max, negate=True)
                v_.tensor_reduce(negmax[:, j % 2, 0, 1:2], prob[:, j % 2, 0, P:3 * P], AX.X, ALU.max, negate=True)\
                    .then_inc(max_ready, 1)

            def shift_scores_odd(n, j):
                dve.wait_ge(consts_ready, 2)
                dve.wait_ge(scores_done, n + 1)
                own.did(v_.tensor_copy(spare, sink_now[:, 0:1]))
                for a, bank in enumerate((ps_s, ps_t)):
                    for t, r in enumerate((slice(0, P), slice(P, 3 * P))):
                        own.did(v_.tensor_tensor_reduce(prob[:, j % 2, a, r], bank[:, r], mask[:, r], 1.0,
                                                        sink_now[:, 2 * j + a:2 * j + a + 1], ALU.subtract, ALU.max,
                                                        rowmax[:, j % 2, a, t:t + 1]))
                own.settle()
                v_.tensor_scalar(negmax[:, j % 2, :, :], rowmax[:, j % 2, :, :], -1.0, None, ALU.mult).then_inc(max_ready, 1)

            def make_y(n, j, odd):
                dve.wait_ge(prob_ready, n + 1)
                dve.wait_ge(pv_done, n + 1)
                na_ = 2 if odd else 1
                if odd:
                    own.did(v_.tensor_tensor(rowsum[:, j % 2, :, :], rowsum[:, j % 2, :, :], esink[:, j % 2, :, :], ALU.add))
                    own.settle()
                own.did(v_.reciprocal(rsum[:, 0:na_, :], rowsum[:, j % 2, 0:na_, :]))
                own.settle()
                w = P // na_
                for a in range(na_):
                    for t in range(T):
                        o = a * w
                        i = v_.scalar_tensor_tensor(out=ysb[:, j % 2, t, o:o + w], in0=ps_o[:, t * P + o:t * P + o + w],
                                                    scalar=rsum[:, a, t:t + 1], in1=gate[:, t, j * P + o:j * P + o + w],
                                                    op0=ALU.mult, op1=ALU.mult)
                i.then_inc(y_ready, 1)

            def y_lo_part(n, kt):
                dve.wait_ge(yhi_ready, n + 1)
                v_.tensor_tensor(y_lo[:, kt, :], ps_o[:, 2 * P:4 * P], y_hi[:, kt, :], ALU.subtract).then_inc(ylo_ready, 1)

            def attention(h, base, slot, kt, odd):
                for j in range(4):
                    if h == YFLIP_AT[j]:
                        y_lo_part(base + j, kt + j)
                for j in range(4):
                    if h == PV_AT[j]:
                        make_y(base + j, j, odd)
                for j in range(4):
                    if h == SCORES_AT[j]:
                        if odd:
                            shift_scores_odd(base + j, j)
                        else:
                            shift_scores_even(base + j, j, slot + j)

            def pick_sinks(group):
                v_.tensor_copy(sink_now, sinks_b[:, bass.ds(group * 8, 8)]).then_inc(sinks_picked, 1)
                dve.wait_ge(sinks_picked, group + 1)

            def add_output(layer, c, done):
                dve.wait_ge(visit_done, done)
                if layer == 0 and c == 0:
                    dve.wait_ge(resid_landed, 16 * OC)
                for t in range(T):
                    r = resid[:, t, c * CW:(c + 1) * CW]
                    i = v_.tensor_tensor(r, ps_proj[2 * ((OUT1 if layer else OUT0) + c) % 4 + t][:, :], r, ALU.add)
                i.then_inc(out_added, 1)

            def output_stage(layer):
                c0 = OUT1 if layer else OUT0
                for v in range(len(OUT_ORDER)):
                    if not (layer and v >= len(OUT_ORDER) - 2):
                        ahead(c0 + v // V, v % V)
                    if v == 0:
                        make_gate(3 + 4 * layer)
                    if layer and v == 0:
                        pick_sinks(3)
                    for h in ((v,) if v < 12 else (12, 13) if v == 12 else (14, 15) if v == 13 else ()):
                        attention(h, 16 * layer + 12, 8, 12, layer == 1)
                    for c, at in enumerate((14, 16, 24)):
                        if v == at:
                            add_output(layer, c, V * c0 + at)
                    if layer == 0:
                        for c, at in enumerate((20, 23, 29)):
                            if v == at:
                                x_lo_part(1, c)

            dve.wait_ge(small_landed, N_SMALL)
            for s in range(2):
                split_lo(0, s, IW)
            for c in range(OC):
                x_lo_part(0, c)
            stream_rstd(0)
            for c in range(GROUP0):
                for s in range(V):
                    ahead(c, s, chunk_width(c + 1))

            ik = ix[:, :, IK:IK + ID]
            iw = ix[:, :, IWT:IWT + IH]
            for part in range(4):
                for s in range(V):
                    h = V * part + s
                    ahead(GROUP0 + part, s)
                    if h == 0:
                        dve.wait_ge(chunk_read, 3)
                        dve.wait_ge(consts_ready, 2)
                        dve.wait_ge(tables_ready, 1)
                        own.did(v_.tensor_tensor(ikn[:, :, 0, :], ik, ik, ALU.mult))
                        own.settle()
                        own.did(v_.tensor_reduce(ssumq[:, 0:T], ikn[:, :, 0, :], AX.X, ALU.add))
                        variance(ssumq[:, 0:T], T, ID)
                        own.did(v_.tensor_tensor(zf, ix[:, :, IAF:IAF + H0], bf_b.unsqueeze(1).to_broadcast([P, T, H0]), ALU.add))
                        own.settle()
                        own.did(v_.tensor_scalar(nzf, zf, -1.0, None, ALU.mult))
                        own.settle()
                        v_.tensor_tensor(azf, zf, nzf, ALU.max).then_inc(gate_abs, 1)
                        own.did(v_.tensor_scalar(mzf, zf, 0.0, None, ALU.min))
                        own.did(v_.tensor_scalar(iw, iw, IH ** -0.5, None, ALU.mult))
                        refine(event_of("ik"), T, rinv[:, 0:T])
                        for t in range(T):
                            i = v_.tensor_scalar(ikn[:, t, 1, :], ik[:, t, :], rinv[:, t:t + 1], None, ALU.mult)
                            own.did(i)
                        own.settle()
                        v_.tensor_tensor(ikn[:, :, 2, :], ikn[:, :, 1, :], tab64_c[:, 1, :, :], ALU.mult).then_inc(ik_read, 1)
                        dve.wait_ge(gate_soft, 1)
                        v_.tensor_tensor(logf, mzf, lzf, ALU.subtract).then_inc(logf_ready, 1)
                    if h == 1:
                        dve.wait_ge(logf_ready, 1)
                        for b in range(2):
                            i = v_.tensor_copy(lf_b[b], logf[:, :, 4 * b:4 * b + 4].unsqueeze(3).to_broadcast([P, T, 4, P]))
                        i.then_inc(lfb_ready, 1)
                    if h == 2:
                        dve.wait_ge(ik_read, 1)
                        dve.wait_ge(ik_swapped, 1)
                        own.did(v_.tensor_tensor(ikn[:, :, 3, :], ikn[:, :, 2, :], ikn[:, :, 0, :], ALU.add))
                        own.settle()
                        v_.tensor_copy(ikn[:, :, 2, :], ikn[:, :, 3, :]).then_inc(ix_roped, 1)
                    if h in (2, 3):
                        t = h - 2
                        q = ix[:, t, 0:IH * ID].rearrange("p (h d) -> p h d", d=ID)
                        m = tmp[:, :, :].rearrange("p t n -> p (t n)").rearrange("p (h d) -> p h d", d=ID)
                        w = (sq, qk)[t][:, :, :].rearrange("p t n -> p (t n)").rearrange("p (h d) -> p h d", d=ID)
                        if t == 1:
                            dve.wait_ge(ix_roped, 2)
                        own.did(v_.tensor_tensor(m, q, tab64_c[:, 0, t, :].unsqueeze(1).to_broadcast([P, IH, ID]), ALU.mult))
                        own.settle()
                        dve.wait_ge(ix_swapped, t + 1)
                        v_.tensor_tensor(q, m, w, ALU.add).then_inc(ix_roped, 1)
                    if h == 4:
                        dve.wait_ge(cq_done, 1)
                        v_.tensor_copy(cq, ps_o[:, 0:2 * H0].rearrange("p (t h) -> p t h", t=T)).then_inc(cq_ready, 1)
                        dve.wait_ge(cq_ready, 1)
                    if h == V + 2:
                        qk_variance(0, 4, HD)
                    if 10 <= h < 14:
                        i0 = h - 10
                        dve.wait_ge(ck_done, i0 + 1)
                        for b in range(2):
                            hh = 2 * i0 + b
                            ck = ps_o[:, b * 2 * P:(b + 1) * 2 * P]
                            v_.scalar_tensor_tensor(out=bias[:, hh, 0:P], in0=ck[:, 0:P], scalar=cq[:, 0, hh:hh + 1],
                                                    in1=mask[:, 0:P], op0=ALU.subtract, op1=ALU.add)
                            v_.tensor_scalar(bias[:, hh, P:2 * P], ck[:, 0:P], cq[:, 1, hh:hh + 1], None, ALU.subtract)
                            i = v_.scalar_tensor_tensor(out=bias[:, hh, 2 * P:3 * P], in0=ck[:, P:2 * P],
                                                        scalar=cq[:, 1, hh:hh + 1], in1=mask[:, 2 * P:3 * P],
                                                        op0=ALU.subtract, op1=ALU.add)
                        i.then_inc(ck_read, 1)
                    if h == V + 3:
                        qk_norm(event_of("even", 0), 4, HD)
                    if h == V + 4:
                        qk_cos(0, 4, HD, tab_c[:, 0])
                    if h == V + 5:
                        qk_rope(0, 4, HD)
                    if 11 <= h < 19:
                        i0 = h - 11
                        dve.wait_ge(relu_ready, i0 + 1)
                        for a in range(2):
                            hh = 2 * i0 + a
                            own.settle()
                            if a == 0 and i0:
                                dve.wait_ge(weighed, i0)
                            for t, r in enumerate((slice(0, P), slice(P, 3 * P))):
                                if hh == 0:
                                    i = v_.tensor_scalar(score[:, r], prob[:, 0, 0, r], iw[:, t, 0:1], None, ALU.mult)
                                else:
                                    i = v_.scalar_tensor_tensor(out=score[:, r], in0=prob[:, i0 % 2, a, r],
                                                                scalar=iw[:, t, hh:hh + 1], in1=score[:, r],
                                                                op0=ALU.mult, op1=ALU.add)
                                if a == 0:
                                    own.did(i)
                        i.then_inc(weighed, 1)
                    if h == 2 * V + 2:
                        qk_variance(1, 4, HD)
                    if h == 2 * V + 3:
                        qk_norm(event_of("even", 1), 4, HD)
                    if h == 2 * V + 4:
                        qk_cos(1, 4, HD, tab_c[:, 1])
                    if h == 2 * V + 5:
                        qk_rope(1, 4, HD)
                    if h == 19:
                        dve.wait_ge(weighed, 8)
                        own.did(v_.tensor_tensor(score[:, 0:P], score[:, 0:P], mask[:, 0:P], ALU.subtract))
                        v_.tensor_tensor(score[:, 2 * P:3 * P], score[:, 2 * P:3 * P], mask[:, 2 * P:3 * P], ALU.subtract)\
                            .then_inc(weighed, 1)
                        dve.wait_ge(weighed, 9)
                    if 20 <= h < 20 + TOPK // 8:
                        for r in (slice(0, P), slice(P, 3 * P)):
                            own.did(v_.max(top8, score[:, r]))
                            own.settle()
                            i = v_.match_replace(score[:, r], top8, score[:, r], TAKEN)
                            if r.start == 0:
                                own.did(i)
                                own.settle()
                        i.then_inc(weighed, 1)
                        dve.wait_ge(weighed, h - 10)
                    if h == 28:
                        for j in range(4):
                            own.did(v_.tensor_scalar(bias[:, 8 + j, :], score[:, :], TAKEN / 2, MASKED, ALU.is_gt, ALU.mult))
                        own.settle()
                        for j in range(4):
                            own.did(v_.tensor_tensor(bias[:, 8 + j, 0:P], bias[:, 8 + j, 0:P], mask[:, 0:P], ALU.max))
                            i = v_.tensor_tensor(bias[:, 8 + j, 2 * P:3 * P], bias[:, 8 + j, 2 * P:3 * P],
                                                 mask[:, 2 * P:3 * P], ALU.max)
                        i.then_inc(weighed, 1)
            dve.wait_ge(ck_read, 4)
            dve.wait_ge(weighed, 18)
            with dve.Fori(0, 3) as turn:
                own.enter(turn, 20)
                c0 = turn * 4 + GROUP0 + 4
                kind = (turn + 1) >> 1
                for part in range(4):
                    for s in range(V):
                        h = V * part + s
                        ahead(c0 + part, s)
                        if h == 0:
                            make_gate(turn)
                        attention(h, turn * 4, turn * 4, turn * 4, False)
                        for b in range(2):
                            if h == (1 + b) * V + 1:
                                qk_variance(turn * 2 + 2 + b, 4, HD)
                            if h == (1 + b) * V + 2:
                                qk_norm(turn * 2 + event_of("even", 2 + b), 4, HD)
                            if h == (1 + b) * V + 3:
                                qk_cos(turn * 2 + 2 + b, 4, HD, tab_c[:, kind * 2 + b])
                            if h == (1 + b) * V + 5:
                                qk_rope(turn * 2 + 2 + b, 4, HD)
                own.leave(3)
            output_stage(0)

            for s in range(V):
                ahead(KV, s)
                if s == 0:
                    add_output(0, 3, V * KV)
                if s == 5:
                    x_lo_part(1, 3)
                    stream_rstd(1)
            for part in range(2):
                for s in range(V):
                    h = V * part + s
                    ahead(SWA0 + part, s)
                    if h == 1:
                        qk_variance(8, SKV, SD)
                    if h == 2:
                        qk_norm(event_of("kv"), SKV, SD)
                    if h == 3:
                        qk_cos(8, SKV, SD, tab64_c[:, 3])
                    if h == 4:
                        qk_rope(8, SKV, SD, twice=True)
                    if h == V + 1:
                        qk_variance(9, 8, SD)
                    if h == V + 2:
                        qk_norm(event_of("odd", 0), 8, SD)
                    if h == V + 3:
                        qk_cos(9, 8, SD, tab64_c[:, 2])
                    if h == V + 4:
                        qk_rope(9, 8, SD)
            with dve.Fori(0, 3) as turn:
                own.enter(turn, 34)
                c0 = turn * 2 + SWA0 + 2
                for part in range(2):
                    for s in range(V):
                        h = V * part + s
                        ahead(c0 + part, s)
                        if h == 0:
                            make_gate(turn + 4)
                            pick_sinks(turn)
                        attention(h, turn * 4 + 16, 0, turn * 4, True)
                        if h == V + 1:
                            qk_variance(turn + 10, 8, SD)
                        if h == V + 2:
                            qk_norm(turn + event_of("odd", 1), 8, SD)
                        if h == V + 3:
                            qk_cos(turn + 10, 8, SD, tab64_c[:, 2])
                        if h == V + 5:
                            qk_rope(turn + 10, 8, SD)
                own.leave(3)
            output_stage(1)
            add_output(1, 3, V * NCH)

        @block.gpsimd
        def _(pool):
            own = Steps(pool, pool_did)
            g = nc.gpsimd
            own.did(g.memset(ident[:, :], 1.0))
            own.did(g.memset(tri, 1.0))
            own.did(g.memset(mask[:, :], 0.0))
            own.settle()
            g.affine_select(out=ident[:, :], in_=ident[:, :], pattern=[[-1, P]], compare_op=ALU.is_equal, fill=0.0,
                            base=0, channel_multiplier=1).then_inc(consts_ready, 1)
            g.memset(one_c, 1.0)
            own.did(g.affine_select(out=tri[:, 0:P], in_=tri[:, 0:P], pattern=[[1, P]], compare_op=ALU.is_ge, fill=0.0,
                                    base=0, channel_multiplier=-1))
            for b in (0, 2):
                own.did(g.affine_select(out=mask[:, b * P:(b + 1) * P], in_=mask[:, b * P:(b + 1) * P], pattern=[[-1, P]],
                                        compare_op=ALU.is_ge, fill=MASKED, base=0, channel_multiplier=1))
            g.affine_select(out=mask[:, P:2 * P], in_=mask[:, P:2 * P], pattern=[[1, P]],
                            compare_op=ALU.is_gt, fill=MASKED, base=0, channel_multiplier=-1).then_inc(consts_ready, 1)
            pool.wait_ge(small_landed, N_SMALL)
            for at in (0, 2 * HD, 4 * HD + ID):
                w = HD if at < 4 * HD else SD
                own.did(g.tensor_scalar(gains[:, at:at + w], gains[:, at:at + w], w ** -0.5, None, ALU.mult))
            own.settle()

            def table(tc, ts, at, dh, rope_at, roped=True, gained=True, signal=None):
                half = dh // 2
                if not roped:
                    own.did(g.tensor_copy(tc, gains[:, at:at + dh].unsqueeze(1).to_broadcast([P, T, dh])))
                    own.did(g.memset(ts, 0.0))
                    return
                cos, sin = rope_sb[:, :, rope_at:rope_at + half], rope_sb[:, :, rope_at + half:rope_at + dh]
                lo, hi = slice(0, half), slice(half, dh)
                if not gained:
                    own.did(g.tensor_copy(tc[:, :, lo], cos))
                    own.did(g.tensor_copy(tc[:, :, hi], cos))
                    own.did(g.tensor_scalar(ts[:, :, lo], sin, -1.0, None, ALU.mult))
                    own.did(g.tensor_copy(ts[:, :, hi], sin))
                    return
                g1 = gains[:, at:at + half].unsqueeze(1).to_broadcast([P, T, half])
                g2 = gains[:, at + half:at + dh].unsqueeze(1).to_broadcast([P, T, half])
                own.did(g.tensor_tensor(tc[:, :, lo], cos, g1, ALU.mult))
                own.did(g.tensor_tensor(tc[:, :, hi], cos, g2, ALU.mult))
                own.did(g.tensor_tensor(ts[:, :, lo], sin, g2, ALU.mult))
                own.did(g.tensor_tensor(ts[:, :, hi], sin, g1, ALU.mult))
                own.settle()
                last = g.tensor_scalar(ts[:, :, lo], ts[:, :, lo], -1.0, None, ALU.mult)
                own.did(last) if signal is None else last.then_inc(signal, 1)

            table(tab64_c[:, 0], tab64_s[:, 0], 0, ID, HD, gained=False)
            table(tab64_c[:, 1], tab64_s[:, 1], 4 * HD, ID, HD)
            table(tab64_c[:, 2], tab64_s[:, 2], 4 * HD + ID, SD, HD)
            table(tab64_c[:, 3], tab64_s[:, 3], 4 * HD + 2 * ID, SD, HD)
            table(tab_c[:, 0], tab_s[:, 0], 0, HD, 0, roped=False)
            table(tab_c[:, 1], tab_s[:, 1], HD, HD, 0, roped=False)
            table(tab_c[:, 2], tab_s[:, 2], 2 * HD, HD, 0)
            table(tab_c[:, 3], tab_s[:, 3], 3 * HD, HD, 0, signal=tables_ready)
            own.settle()
            pool.wait_ge(tables_ready, 1)

            pool.wait_ge(chunk_read, 3)
            half = ID // 2
            for t in range(T):
                q = ix[:, t, 0:IH * ID].rearrange("p (h d) -> p h d", d=ID)
                w = (sq, qk)[t][:, :, :].rearrange("p t n -> p (t n)").rearrange("p (h d) -> p h d", d=ID)
                for a, b in ((0, half), (half, 0)):
                    s_ = tab64_s[:, 0, t, a:a + half].unsqueeze(1).to_broadcast([P, IH, half])
                    i = g.tensor_tensor(w[:, :, a:a + half], q[:, :, b:b + half], s_, ALU.mult)
                i.then_inc(ix_swapped, 1)
                if t == 0:
                    pool.wait_ge(ik_read, 1)
                    g.tensor_tensor(ikn[:, :, 0, 0:half], ikn[:, :, 1, half:ID], tab64_s[:, 1, :, 0:half], ALU.mult)
                    g.tensor_tensor(ikn[:, :, 0, half:ID], ikn[:, :, 1, 0:half], tab64_s[:, 1, :, half:ID], ALU.mult)\
                        .then_inc(ik_swapped, 1)

            def swap(k, nh, dh, table):
                pool.wait_ge(qk_normed, k + 1)
                h = dh // 2
                src = qk[:, :, :].rearrange("p t n -> p (t n)")[:, 0:T * nh * dh].rearrange("p (t h d) -> p t h d", t=T, d=dh)
                dst = sq[:, :, :].rearrange("p t n -> p (t n)")[:, 0:T * nh * dh].rearrange("p (t h d) -> p t h d", t=T, d=dh)
                g.tensor_tensor(dst[:, :, :, 0:h], src[:, :, :, h:dh],
                                table[:, :, 0:h].unsqueeze(2).to_broadcast([P, T, nh, h]), ALU.mult)
                g.tensor_tensor(dst[:, :, :, h:dh], src[:, :, :, 0:h],
                                table[:, :, h:dh].unsqueeze(2).to_broadcast([P, T, nh, h]), ALU.mult).then_inc(qk_swapped, 1)

            swap(0, 4, HD, tab_s[:, 0])
            swap(1, 4, HD, tab_s[:, 1])
            with pool.Fori(0, 3) as turn:
                kind = (turn + 1) >> 1
                for b in range(2):
                    swap(turn * 2 + 2 + b, 4, HD, tab_s[:, kind * 2 + b])
            swap(8, SKV, SD, tab64_s[:, 3])
            swap(9, 8, SD, tab64_s[:, 2])

            def pick(group):
                if not isinstance(group, int) or group >= 1:
                    pool.wait_ge(pv_done, group * 4 + 16)
                else:
                    pool.wait_ge(qkT_ready, 18)
                    pool.wait_ge(vals_ready, 5)
                g.tensor_copy(kT_now[:, :], kT[:, group, :]).then_inc(kv_picked, 1)
                g.tensor_copy(v_now[:, :, :], vals[:, :, bass.ds(group * SD, SD)]).then_inc(kv_picked, 1)

            pick(0)
            with pool.Fori(0, 3) as turn:
                swap(turn + 10, 8, SD, tab64_s[:, 2])
                pick(turn + 1)


_INS = ["x", "norm_even", "w_in_even", "b_f_even", "g_qk_fox", "g_qk_dsa", "g_kidx", "w_out_even",
        "norm_odd", "w_in_odd", "g_qk_swa", "sinks", "w_out_odd"]


def rope_constants(seq, dims=(128, 64), theta=10000.0):
    import numpy as np
    parts = []
    for dim in dims:
        inv = (np.float32(1.0) / np.float32(theta) ** (np.arange(0, dim, 2, dtype=np.float32) / np.float32(dim))).astype(np.float32)
        ang = (np.arange(seq, dtype=np.float32)[:, None] * inv[None, :]).astype(np.float32)
        parts += [np.cos(ang.astype(np.float64)), np.sin(ang.astype(np.float64))]
    return np.concatenate(parts, axis=1).astype(np.float32)


def kernel(**inputs):
    import numpy as _np
    import concourse.bacc as _bacc
    from concourse import mybir as _mybir
    from concourse.bass_utils import run_bass_kernel_spmd as _run

    nc = _bacc.Bacc("TRN2", target_bir_lowering=False, num_devices=1)
    arrays, args = {}, []
    for name in _INS:
        a = _np.ascontiguousarray(inputs[name])
        arrays[f"in_{name}"] = a
        args.append(nc.dram_tensor(f"in_{name}", a.shape, _mybir.dt.from_np(a.dtype), kind="ExternalInput").ap())
    shape = tuple(inputs["x"].shape)
    table = rope_constants(shape[1])
    arrays["rope_table"] = table
    args.append(nc.dram_tensor("rope_table", table.shape, _mybir.dt.float32, kind="ExternalInput").ap())
    args.append(nc.dram_tensor("out_0", shape, _mybir.dt.float32, kind="ExternalOutput").ap())
    hybrid_trunk(nc, *args)
    r = _run(nc, [arrays], core_ids=[0])
    return r.results[0]["out_0"]
```

```python
from contextlib import ExitStack

import concourse.bass as bass
from concourse import mybir

F32 = mybir.dt.float32
F32R = mybir.dt.float32r
ALU = mybir.AluOpType
ACT = mybir.ActivationFunctionType
AX = mybir.AxisListType

P = 128
T = 2
CW = 512
VK = 2
RAW = 4
HL = 4
LEAD = HL - 1
EPS = 1e-6
MASKED = 1e30
TAKEN = -3e38

BESIDE = (([1, 4, 7, 10], [3, 6, 9, 12], [4, 7, 10, 13], [5, 8, 11, 14]),
          ([0, 3, 6, 9], [2, 5, 8, 11], [3, 6, 9, 12], [5, 7, 10, 13]))
AT_END = (([0, 2, 4, 6], [2, 4, 6, 8], [3, 5, 7, 9], [4, 6, 8, 10]),
          ([-1, 2, 5, 8], [1, 4, 7, 10], [2, 5, 8, 11], [4, 7, 10, 12]))


class Steps:

    def __init__(self, eng, sem):
        self.eng, self.sem, self.n, self.base = eng, sem, 0, 0

    def did(self, instruction):
        instruction.then_inc(self.sem, 1)
        self.n += 1

    def settle(self):
        self.eng.wait_ge(self.sem, self.base + self.n)

    def enter(self, turn, per_turn):
        self.base, self.start, self.per = turn * per_turn, self.n, per_turn

    def leave(self, turns):
        assert self.n - self.start == self.per, (self.sem, self.n - self.start)
        self.n, self.base = self.start + self.per * turns, 0


def hybrid_trunk(nc, x, norm_even, w_in_even, b_f_even, g_qk_fox, g_qk_dsa, g_kidx, w_out_even,
                 norm_odd, w_in_odd, g_qk_swa, sinks, w_out_odd, rope, out):
    D = x.shape[2]
    KT = D // P
    OC = D // CW
    V = KT // VK
    EVEN = w_in_even.shape[2]
    H0, HD = 8, 128
    IH, ID = 16, 64
    SH, SKV, SD = 32, 4, 64
    TOPK = x.shape[1] // 4
    FW = H0 * HD
    AF = 4 * FW
    DSA = AF + H0
    IQ = DSA + 4 * FW
    IW = (EVEN - IQ) // 3
    IXW = IH * ID + ID + IH + H0
    IK, IWT, IAF = IH * ID, IH * ID + ID, IH * ID + ID + IH
    assert IW * 3 == EVEN - IQ and KT == 16 and OC == 4
    GROUP0 = 3
    OUT0 = GROUP0 + 16
    KV = OUT0 + OC
    SWA0 = KV + 1
    OUT1 = SWA0 + 8
    NCH = OUT1 + OC
    OUT_ORDER = ([(0, s) for s in range(6)] + [(1, s) for s in range(6)] + [(0, 6), (1, 6), (0, 7), (1, 7)]
                 + [(c, s) for c in (2, 3) for s in range(8)])

    ctx = ExitStack()
    with ctx:
        def sb(name, shape, dt=F32):
            return ctx.enter_context(nc.sbuf_tensor(name, shape, dt))

        def sem(name):
            return ctx.enter_context(nc.semaphore(name))

        x_hi, x_lo = sb("x_hi", [P, KT, T * P], F32R), sb("x_lo", [P, KT, T * P], F32R)
        y_hi, y_lo = sb("y_hi", [P, KT, T * P], F32R), sb("y_lo", [P, KT, T * P], F32R)
        w_raw = sb("w_raw", [P, RAW, VK, CW])
        w_hi, w_lo = sb("w_hi", [P, HL, VK, CW], F32R), sb("w_lo", [P, HL, VK, CW], F32R)
        resid = sb("resid", [P, T, D])
        ixT = sb("ixT", [P, 8, T * P])
        bias = sb("bias", [P, 12, 3 * P])
        tab_c, tab_s = sb("tab_c", [P, 6, T, HD]), sb("tab_s", [P, 6, T, HD])
        tab64_c, tab64_s = (t[:, 4:6, :, :].rearrange("p a t (b d) -> p (a t b d)", b=2)
                            .rearrange("p (k t d) -> p k t d", k=4, t=T) for t in (tab_c, tab_s))
        qk = sb("qk", [P, T, CW])
        sq = sb("sq", [P, T, CW])
        tmp = sb("tmp", [P, T, CW])
        vals = sb("vals", [P, T, CW])
        gate = sb("gate", [P, T, CW])
        qT, kT = sb("qT", [P, 4, T * P]), sb("kT", [P, 4, T * P])
        prob = sb("prob", [P, 2, 2, 3 * P])
        ysb = sb("ysb", [P, 2, T, P])
        kT_now, v_now = sb("kT_now", [P, T * P]), sb("v_now", [P, T, SD])
        ident = sb("ident", [P, P])
        mask = sb("mask", [P, 3 * P])
        norms = sb("norms", [P, 2 * KT])
        small = sb("small", [P, 384])
        col = iter(range(0, 384))

        def cols(n):
            a = [next(col) for _ in range(n)][0]
            return small[:, a:a + n]
        one_c = cols(1)
        ssq = cols(8).rearrange("p (t c) -> p t c", t=T)
        ssum = cols(T)
        var, lnv, r0, na, nb, rinv = (cols(16) for _ in range(6))
        rstd, nrstd = cols(T), cols(T)
        negmax = cols(8).rearrange("p (b a t) -> p b a t", b=2, a=2)
        rowmax = cols(8).rearrange("p (b a t) -> p b a t", b=2, a=2)
        rowsum = cols(8).rearrange("p (b a t) -> p b a t", b=2, a=2)
        esink = cols(8).rearrange("p (b a t) -> p b a t", b=2, a=2)
        sinkdiff = cols(8).rearrange("p (b a t) -> p b a t", b=2, a=2)
        rsum = cols(4).rearrange("p (a t) -> p a t", a=2)
        sink_now = cols(8)
        sinks_b = cols(SH)
        bf_b = cols(H0)
        zf, nzf, azf, mzf, ezf, lzf, logf = (cols(T * H0).rearrange("p (t h) -> p t h", t=T) for _ in range(7))
        cq = cols(T * H0).rearrange("p (t h) -> p t h", t=T)
        top8 = cols(T * 8).rearrange("p (t n) -> p t n", t=T)
        ssumq = cols(16)
        spare = cols(1)
        tri = ysb[:, :, :, :].rearrange("p b t n -> p (b t n)")[:, 0:2 * P]
        norm_rows = qT[0:2 * KT, 0, 0:P]
        rope_sb = kT[:, :, :].rearrange("p h n -> p (h n)")[:, 0:T * (HD + SD)].rearrange("p (t n) -> p t n", t=T)
        probT = ixT[:, :, :].rearrange("p h n -> p (h n)")[:, 0:2 * 3 * P].rearrange("p (a n) -> p a n", a=2)
        ix = resid[:, :, :].rearrange("p t d -> p (t d)")[:, 0:T * IXW].rearrange("p (t n) -> p t n", t=T)
        score = resid[:, :, :].rearrange("p t d -> p (t d)")[:, T * IXW:T * IXW + 3 * P]
        ikn = resid[:, :, :].rearrange("p t d -> p (t d)")[:, T * IXW + 3 * P:T * IXW + 3 * P + 512].rearrange(
            "p (t a d) -> p t a d", t=T, a=4)
        ikT = kT_now
        gains = qk[:, :, :].rearrange("p t n -> p (t n)")
        lf_b = [vals[:, :, :].rearrange("p t (h n) -> p t h n", h=4), gate[:, :, :].rearrange("p t (h n) -> p t h n", h=4)]

        ps_proj = [ctx.enter_context(nc.psum_tensor(f"ps_proj{i}", [P, CW], F32)) for i in range(4)]
        ps_s = ctx.enter_context(nc.psum_tensor("ps_s", [P, CW], F32))
        ps_t = ctx.enter_context(nc.psum_tensor("ps_t", [P, CW], F32))
        ps_p = ctx.enter_context(nc.psum_tensor("ps_p", [P, CW], F32))
        ps_o = ctx.enter_context(nc.psum_tensor("ps_o", [P, CW], F32))

        x_landed = [sem(f"x_landed{i}") for i in range(KT // 2)]
        small_landed, norms_landed = sem("small_landed"), sem("norms_landed")
        resid_landed = sem("resid_landed")
        w_landed = [sem(f"w_landed{i}") for i in range(RAW)]
        out_stored = sem("out_stored")
        hi_ready, lo_ready, visit_done = sem("hi_ready"), sem("lo_ready"), sem("visit_done")
        chunk_read = sem("chunk_read")
        out_added = sem("out_added")
        consts_ready = sem("consts_ready")
        tables_ready = sem("tables_ready")
        norms_flipped, norms_ready = sem("norms_flipped"), sem("norms_ready")
        x_flipped, xhi_ready, xlo_ready = sem("x_flipped"), sem("xhi_ready"), sem("xlo_ready")
        squares_ready = sem("squares_ready")
        var_ready, root_ready = sem("var_ready"), sem("root_ready")
        rstd_ready = sem("rstd_ready")
        qk_read, qk_normed, qk_swapped, qk_ready = sem("qk_read"), sem("qk_normed"), sem("qk_swapped"), sem("qk_ready")
        qk_flipped, qkT_ready = sem("qk_flipped"), sem("qkT_ready")
        vals_ready, sig_ready, gate_ready = sem("vals_ready"), sem("sig_ready"), sem("gate_ready")
        scores_done, max_ready, prob_ready = sem("scores_done"), sem("max_ready"), sem("prob_ready")
        prob_flipped, probT_ready = sem("prob_flipped"), sem("probT_ready")
        pv_done, y_ready, y_flipped, yhi_ready, ylo_ready = (
            sem("pv_done"), sem("y_ready"), sem("y_flipped"), sem("yhi_ready"), sem("ylo_ready"))
        kv_picked, sinks_picked = sem("kv_picked"), sem("sinks_picked")
        ix_swapped, ix_roped, ix_flipped, ixT_ready = sem("ix_swapped"), sem("ix_roped"), sem("ix_flipped"), sem("ixT_ready")
        ik_swapped, ik_read = sem("ik_swapped"), sem("ik_read")
        logits_done, relu_ready, weighed = sem("logits_done"), sem("relu_ready"), sem("weighed")
        gate_abs, gate_soft, logf_ready, lfb_ready = sem("gate_abs"), sem("gate_soft"), sem("logf_ready"), sem("lfb_ready")
        cq_done, cq_ready, ck_done, ck_read = sem("cq_done"), sem("cq_ready"), sem("ck_done"), sem("ck_read")
        dve_did, act_did, pool_did = sem("dve_did"), sem("act_did"), sem("pool_did")

        w0 = w_in_even[0].rearrange("(k p) n -> p k n", p=P)
        w1 = w_in_odd[0].rearrange("(k p) n -> p k n", p=P)
        wo0 = w_out_even[0].rearrange("(k p) n -> p k n", p=P)
        wo1 = w_out_odd[0].rearrange("(k p) n -> p k n", p=P)
        x_dram = x[0].rearrange("(t p) d -> p t d", p=P)
        out_dram = out[0].rearrange("(t p) d -> p t d", p=P)
        rope_dram = rope.rearrange("(t p) d -> p t d", p=P)
        N_SMALL = 16 * 7

        def chunk_width(c):
            return (IW, IW, IW + H0)[c] if isinstance(c, int) and c < GROUP0 else CW

        def landed_count(c, s):
            turns = 2 * c + s // RAW
            if isinstance(c, int) and c < GROUP0:
                return 16 * (turns + 1) + (16 * (turns - 3) if c == 2 else 0)
            return 16 * (turns + 1) + 32

        def event_of(kind, k=0):
            return {"rstd0": 0, "ik": 1, "even": 2 + k, "rstd1": 10, "kv": 11, "odd": 12 + k}[kind]

        block = ctx.enter_context(nc.Block())

        @block.sync
        def _(sp):
            def load_x(i):
                r = slice(i * 2 * P, (i + 1) * 2 * P)
                sp.dma_start(resid[:, :, r], x_dram[:, :, r]).then_inc(x_landed[i], 16)

            def weights(c, s, src, first_col, width=CW, at=0, k_tile=None):
                k = VK * s if k_tile is None else k_tile
                return sp.dma_start(w_raw[:, s % RAW, :, at:at + width],
                                    src[:, k:k + VK, bass.ds(first_col, width)]).then_inc(w_landed[s % RAW], 16)

            def ring_free(c, s):
                if not isinstance(c, int) or V * c + s >= RAW:
                    sp.wait_ge(lo_ready, V * c + s - RAW + 1)

            for c in range(GROUP0):
                for s in range(V):
                    if c == 0:
                        load_x(s)
                    ring_free(c, s)
                    weights(c, s, w0, IQ + IW * c, IW)
                    if c == GROUP0 - 1:
                        weights(c, s, w0, AF, H0, at=IW)
            with sp.Fori(0, 2) as kind:
                with sp.Fori(0, 2) as half:
                    with sp.Fori(0, 4) as part:
                        for s in range(V):
                            c = kind * 8 + half * 4 + part + GROUP0
                            ring_free(c, s)
                            weights(c, s, w0, kind * DSA + half * CW + part * FW)
            sp.wait_ge(weighed, 9 + 9)
            for c in range(OC):
                sp.dma_start(resid[:, :, c * CW:(c + 1) * CW], x_dram[:, :, c * CW:(c + 1) * CW]).then_inc(resid_landed, 16)
            for v, (c, s) in enumerate(OUT_ORDER):
                ring_free(OUT0 + v // V, v % V)
                weights(OUT0, v % V, wo0, c * CW, k_tile=VK * s)
            for s in range(V):
                ring_free(KV, s)
                weights(KV, s, w1, SH * SD)
            with sp.Fori(0, 4) as group:
                for part in range(2):
                    for s in range(V):
                        c = group * 2 + part + SWA0
                        ring_free(c, s)
                        weights(c, s, w1, group * CW + part * (SH * SD + 2 * SKV * SD))
            for v, (c, s) in enumerate(OUT_ORDER):
                ring_free(OUT1 + v // V, v % V)
                weights(OUT1, v % V, wo1, c * CW, k_tile=VK * s)
            for c in range(OC - 1):
                sp.wait_ge(out_added, OC + c + 1)
                sp.dma_start(out_dram[:, :, c * CW:(c + 1) * CW], resid[:, :, c * CW:(c + 1) * CW]).then_inc(out_stored, 16)
            for t in range(T):
                sp.wait_ge(out_added, 2 * OC + t)
                sp.dma_start(out_dram[:, t, (OC - 1) * CW:], resid[:, t, (OC - 1) * CW:]).then_inc(out_stored, 16)
            sp.wait_ge(out_stored, 16 * (OC + 1))

        @block.tensor
        def _(pe):
            BY_K = [(k, t) for k in range(VK) for t in range(T)]
            BY_TOKENS = [(k, t) for t in range(T) for k in range(VK)]

            def project(c, s, bank, acts_hi, acts_lo, kt=None, width=CW, first=False, last=False, tiles=BY_K):
                k0 = VK * s if kt is None else kt
                pe.wait_ge(lo_ready, V * c + s + 1)
                for k, t in tiles:
                    o = ps_proj[2 * bank + t][:, 0:width]
                    a_hi = acts_hi[:, k0 + k, t * P:(t + 1) * P]
                    a_lo = acts_lo[:, k0 + k, t * P:(t + 1) * P]
                    h, l = w_hi[:, s % HL, k, 0:width], w_lo[:, s % HL, k, 0:width]
                    nc.tensor.matmul(o, a_hi, h, start=first and k == 0, stop=False)
                    nc.tensor.matmul(o, a_hi, l, start=False, stop=False)
                    mm = nc.tensor.matmul(o, a_lo, h, start=False, stop=last and k == VK - 1)
                    if tiles is BY_TOKENS and (k, t) == (VK - 1, 0):
                        mm.then_inc(visit_done, 1)
                mm.then_inc(visit_done, 1)

            def chunk_visit(c, s, bank, free=None, width=CW):
                if s == 0 and free is not None:
                    pe.wait_ge(*free)
                if isinstance(c, int) and c in (0, KV):
                    pe.wait_ge(xlo_ready, (V if c else 0) + s + 1)
                project(c, s, bank, x_hi, x_lo, width=width, first=s == 0, last=s == V - 1)

            def flip_x(layer, c):
                banks = (ps_s, ps_t) if c % 2 == 0 else (ps_p, ps_o)
                if layer:
                    pe.wait_ge(out_added, c + 1)
                if c >= 2:
                    pe.wait_ge(xlo_ready, V * layer + 2 * (c - 1))
                for k in range(4):
                    if layer == 0 and k % 2 == 0:
                        pe.wait_ge(x_landed[2 * c + k // 2], 16)
                    for t in range(T):
                        a = (k % 2) * 2 * P + t * P
                        mm = nc.tensor.transpose(banks[k // 2][:, a:a + P],
                                                 resid[:, t, c * CW + k * P:c * CW + (k + 1) * P], ident[:, :])
                    if k % 2:
                        mm.then_inc(x_flipped, 1)

            def flip_qk(step, half):
                pe.wait_ge(qk_ready, step // 2 + 1)
                if not isinstance(step, int) or step >= 1:
                    pe.wait_ge(qkT_ready, step)
                for b in range(2):
                    for t in range(T):
                        a = b * 2 * P + t * P
                        mm = nc.tensor.transpose(ps_t[:, a:a + P], qk[:, t, (2 * half + b) * P:(2 * half + b + 1) * P],
                                                 ident[:, :])
                mm.then_inc(qk_flipped, 1)

            def scores_even(n, j, group):
                if j == 0:
                    pe.wait_ge(qkT_ready, 4 * (group + 1))
                nc.tensor.matmul(ps_s[:, 0:P], qT[:, j, 0:P], kT[:, j, 0:P], start=True, stop=True)
                nc.tensor.matmul(ps_s[:, P:3 * P], qT[:, j, P:2 * P], kT[:, j, :], start=True, stop=True)\
                    .then_inc(scores_done, 1)

            def scores_odd(n, j, group):
                if j == 0:
                    pe.wait_ge(qkT_ready, 16 + 2 + 2 * (group + 1))
                    pe.wait_ge(kv_picked, 2 * (group + 1))
                for a, bank in enumerate((ps_s, ps_t)):
                    r = slice(a * SD, (a + 1) * SD)
                    nc.tensor.matmul(bank[:, 0:P], qT[r, j, 0:P], kT_now[r, 0:P], start=True, stop=True)
                    mm = nc.tensor.matmul(bank[:, P:3 * P], qT[r, j, P:2 * P], kT_now[r, :], start=True, stop=True)
                mm.then_inc(scores_done, 1)

            def flip_prob(n, j, odd):
                pe.wait_ge(prob_ready, n + 1)
                for a in range(2 if odd else 1):
                    bank = (ps_p, ps_s)[a]
                    for b in range(3):
                        mm = nc.tensor.transpose(bank[:, b * P:(b + 1) * P], prob[:, j % 2, a, b * P:(b + 1) * P],
                                                 ident[:, :])
                mm.then_inc(prob_flipped, 1)

            def pv_even(n, j, group):
                pe.wait_ge(probT_ready, n + 1)
                if j == 0:
                    pe.wait_ge(vals_ready, group + 1)
                else:
                    pe.wait_ge(ylo_ready, n)
                v = [vals[:, t, j * P:(j + 1) * P] for t in range(T)]
                nc.tensor.matmul(ps_o[:, 0:P], probT[:, 0, 0:P], v[0], start=True, stop=True)
                nc.tensor.matmul(ps_o[:, P:2 * P], probT[:, 0, P:2 * P], v[0], start=True, stop=False)
                nc.tensor.matmul(ps_o[:, P:2 * P], probT[:, 0, 2 * P:3 * P], v[1], start=False, stop=True)\
                    .then_inc(pv_done, 1)

            def pv_odd(n, j, group):
                pe.wait_ge(probT_ready, n + 1)
                if j:
                    pe.wait_ge(ylo_ready, n)
                for a in range(2):
                    o = [ps_o[:, t * P + a * SD:t * P + (a + 1) * SD] for t in range(T)]
                    nc.tensor.matmul(o[0], probT[:, a, 0:P], v_now[:, 0, :], start=True, stop=True)
                    nc.tensor.matmul(o[1], probT[:, a, P:2 * P], v_now[:, 0, :], start=True, stop=False)
                    mm = nc.tensor.matmul(o[1], probT[:, a, 2 * P:3 * P], v_now[:, 1, :], start=False, stop=True)
                mm.then_inc(pv_done, 1)

            def flip_y(n, j):
                pe.wait_ge(y_ready, n + 1)
                for t in range(T):
                    mm = nc.tensor.transpose(ps_o[:, 2 * P + t * P:2 * P + (t + 1) * P], ysb[:, j % 2, t, :], ident[:, :])
                mm.then_inc(y_flipped, 1)

            def attention(h, base, group, odd, stages=BESIDE):
                at = stages[odd]
                """What of the group's attention comes after visit h of the body."""
                for j in range(4):
                    if h == at[3][j]:
                        flip_y(base + j, j)
                for j in range(4):
                    if h == at[2][j]:
                        (pv_odd if odd else pv_even)(base + j, j, group)
                for j in range(4):
                    if h == at[1][j]:
                        flip_prob(base + j, j, odd)
                for j in range(4):
                    if h == at[0][j]:
                        (scores_odd if odd else scores_even)(base + j, j, group)

            def output_stage(layer):
                c0 = OUT1 if layer else OUT0
                base = 16 * layer + 12
                for v, (c, s) in enumerate(OUT_ORDER):
                    if v == 0:
                        pe.wait_ge(*((qk_read, 13) if layer else (vals_ready, 4)))
                    if v == 6:
                        pe.wait_ge(gate_ready, 4 * layer + 4)
                    if s == 0 and c >= 2:
                        pe.wait_ge(out_added, OC * layer + c - 1)
                    if v == 0:
                        attention(-1, base, 3, layer == 1, AT_END)
                        pe.wait_ge(ylo_ready, base)
                    if s == 6 and c < 2:
                        pe.wait_ge(ylo_ready, base + 2)
                    if s == 7 and c < 2:
                        pe.wait_ge(ylo_ready, base + 4)
                    if layer == 0 and v == 20:
                        flip_x(1, 0)
                    if layer == 0 and v == 23:
                        flip_x(1, 1)
                    if layer == 0 and v == 29:
                        flip_x(1, 2)
                    project(c0 + v // V, v % V, (c0 + c) % 2, y_hi, y_lo, kt=VK * s, first=s == 0, last=s == V - 1,
                            tiles=BY_TOKENS if layer and v == len(OUT_ORDER) - 1 else BY_K)
                    if v < 14:
                        attention(v, base, 3, layer == 1, AT_END)

            pe.wait_ge(consts_ready, 1)
            pe.wait_ge(norms_landed, 2 * 16)
            nc.tensor.transpose(ps_proj[3][:, 0:2 * KT], norm_rows, ident[0:2 * KT, 0:2 * KT]).then_inc(norms_flipped, 1)
            flip_x(0, 0)
            for c in range(GROUP0):
                for s in range(V):
                    if c == 0 and s in (1, 3, 5):
                        flip_x(0, (s + 1) // 2)
                    free = (None, (norms_ready, 1), (chunk_read, 1))[c]
                    chunk_visit(c, s, c % 2, free, chunk_width(c))

            pe.wait_ge(consts_ready, 2)
            for part in range(4):
                for s in range(V):
                    h = V * part + s
                    chunk_visit(GROUP0 + part, s, (GROUP0 + part) % 2, ((chunk_read, 2), (chunk_read, 3), (qk_read, 1), (qk_read, 2))[part])
                    if h == 3:
                        pe.wait_ge(logf_ready, 1)
                        nc.tensor.matmul(ps_o[:, 0:H0], tri[:, 0:P], logf[:, 0, :], start=True, stop=True)
                        nc.tensor.matmul(ps_o[:, H0:2 * H0], tri[:, P:2 * P], logf[:, 0, :], start=True, stop=False)
                        nc.tensor.matmul(ps_o[:, H0:2 * H0], tri[:, 0:P], logf[:, 1, :], start=False, stop=True)\
                            .then_inc(cq_done, 1)
                    if 5 <= h < 9:
                        i = h - 5
                        pe.wait_ge(ix_roped, 3)
                        if i == 3:
                            pe.wait_ge(cq_ready, 1)
                        bank = (ps_s, ps_t, ps_p, ps_o)[i]
                        for b in range(2):
                            for t in range(T):
                                a = b * 2 * P + t * P
                                mm = nc.tensor.transpose(bank[:, a:a + P], ix[:, t, (2 * i + b) * P:(2 * i + b + 1) * P],
                                                         ident[:, :])
                        mm.then_inc(ix_flipped, 1)
                    if h == 9:
                        pe.wait_ge(ixT_ready, 2)
                        for t in range(T):
                            mm = nc.tensor.transpose(ps_t[:, t * P:(t + 1) * P],
                                                     ikn[:, t, 2:4, :].rearrange("p a d -> p (a d)"), ident[:, :])
                        mm.then_inc(ix_flipped, 1)
                    if 10 <= h < 14:
                        i = h - 10
                        pe.wait_ge(lfb_ready, 1)
                        pe.wait_ge(ixT_ready, 4)
                        if i >= 1:
                            pe.wait_ge(ck_read, i)
                        for b in range(2):
                            hh = 2 * i + b
                            lf = lf_b[hh // 4]
                            o = ps_o[:, b * 2 * P:(b + 1) * 2 * P]
                            nc.tensor.matmul(o, lf[:, 0, hh % 4, :], tri, start=True, stop=False)
                            mm = nc.tensor.matmul(o[:, P:2 * P], lf[:, 1, hh % 4, :], tri[:, 0:P], start=False, stop=True)
                        mm.then_inc(ck_done, 1)
                    if 11 <= h < 19:
                        i = h - 11
                        pe.wait_ge(ixT_ready, 5)
                        if i >= 1:
                            pe.wait_ge(relu_ready, i)
                        for a, bank in enumerate((ps_s, ps_p)):
                            r = slice(a * ID, (a + 1) * ID)
                            nc.tensor.matmul(bank[:, 0:P], ixT[r, i, 0:P], ikT[r, 0:P], start=True, stop=True)
                            mm = nc.tensor.matmul(bank[:, P:3 * P], ixT[r, i, P:2 * P], ikT[r, :], start=True, stop=True)
                        mm.then_inc(logits_done, 1)
                    if h in (14, 15):
                        flip_qk(h - 14, h - 14)
                    if h in (27, 28):
                        flip_qk(h - 25, h - 27)
            pe.wait_ge(relu_ready, 8)
            pe.wait_ge(ck_read, 4)
            with pe.Fori(0, 3) as turn:
                for part in range(4):
                    for s in range(V):
                        h = V * part + s
                        free = ((vals_ready, turn + 1), (gate_ready, turn + 1), (qk_read, turn * 2 + 3),
                                (qk_read, turn * 2 + 4))[part]
                        chunk_visit(turn * 4 + part + GROUP0 + 4, s, (GROUP0 + part) % 2, free)
                        attention(h, turn * 4, turn, False)
                        if h in (15, 16):
                            flip_qk(turn * 4 + 4 + h - 15, h - 15)
                        if h in (23, 24):
                            flip_qk(turn * 4 + 6 + h - 23, h - 23)
            output_stage(0)

            for s in range(V):
                if s == 4:
                    flip_x(1, 3)
                chunk_visit(KV, s, KV % 2, (out_added, OC - 1))
            for part in range(2):
                for s in range(V):
                    h = V * part + s
                    chunk_visit(SWA0 + part, s, part, ((out_added, OC), (vals_ready, 5))[part])
                    if h in (5, 6):
                        flip_qk(16 + h - 5, h - 5)
                    if h in (13, 15):
                        flip_qk(18 + (h - 13) // 2, (h - 13) // 2)
            with pe.Fori(0, 3) as turn:
                for part in range(2):
                    for s in range(V):
                        h = V * part + s
                        chunk_visit(turn * 2 + part + SWA0 + 2, s, part, ((qk_read, turn + 10), (gate_ready, turn + 5))[part])
                        attention(h, turn * 4 + 16, turn, True)
                        if h in (14, 15):
                            flip_qk(turn * 2 + 20 + h - 14, h - 14)
            output_stage(1)

        @block.scalar
        def _(act):
            own = Steps(act, act_did)

            def split_hi(c, s, width=CW):
                act.wait_ge(w_landed[s % RAW], landed_count(c, s))
                if not isinstance(c, int) or V * c + s >= HL:
                    act.wait_ge(visit_done, V * c + s - HL + 1)
                nc.scalar.activation(w_hi[:, s % HL, :, 0:width], w_raw[:, s % RAW, :, 0:width], ACT.Copy)\
                    .then_inc(hi_ready, 1)

            def ahead(c, s, next_width=CW):
                if s < V - LEAD:
                    split_hi(c, s + LEAD, chunk_width(c))
                else:
                    split_hi(c + 1, s + LEAD - V, next_width)

            def x_hi_part(layer, c):
                banks = (ps_s, ps_t) if c % 2 == 0 else (ps_p, ps_o)
                for k in range(4):
                    kt = 4 * c + k
                    if k % 2 == 0:
                        act.wait_ge(x_flipped, V * layer + 2 * c + k // 2 + 1)
                    i = nc.scalar.activation(x_hi[:, kt, :], banks[k // 2][:, (k % 2) * 2 * P:(k % 2 + 1) * 2 * P],
                                             ACT.Copy, scale=norms[:, KT * layer + kt:KT * layer + kt + 1])
                    if k % 2:
                        i.then_inc(xhi_ready, 1)

            def squares(layer, c):
                if OC * layer + c:
                    act.wait_ge(squares_ready, OC * layer + c)
                for t in range(T):
                    i = nc.scalar.activation(tmp[:, t, :], resid[:, t, c * CW:(c + 1) * CW], ACT.Square,
                                             accum_out=ssq[:, t, c:c + 1])
                i.then_inc(squares_ready, 1)

            def root(e, n):
                act.wait_ge(var_ready, e + 1)
                own.did(nc.scalar.activation(lnv[:, 0:n], var[:, 0:n], ACT.Ln))
                own.settle()
                nc.scalar.activation(r0[:, 0:n], lnv[:, 0:n], ACT.Exp, scale=-0.5).then_inc(root_ready, 1)

            def read_index(c):
                act.wait_ge(visit_done, V * (c + 1))
                if c == 0:
                    act.wait_ge(rstd_ready, 1)
                width = chunk_width(c)
                for t in range(T):
                    i = nc.scalar.activation(ix[:, t, IW * c:IW * c + width], ps_proj[2 * (c % 2) + t][:, 0:width],
                                             ACT.Copy, scale=rstd[:, t:t + 1])
                i.then_inc(chunk_read, 1)

            def read_qk(c, bank, width, k, settled):
                act.wait_ge(visit_done, (c + 1) * V)
                if not isinstance(k, int) or k >= 1:
                    act.wait_ge(qk_flipped, 2 * k)
                if settled is not None:
                    act.wait_ge(gate_ready, settled)
                for t in range(T):
                    ps = ps_proj[2 * bank + t][:, 0:width]
                    if width == CW:
                        q_to, s_to = qk[:, t, :], sq[:, t, :]
                    else:
                        q_to, s_to = (b[:, :, :].rearrange("p t n -> p (t n)")[:, t * width:(t + 1) * width] for b in (qk, sq))
                    nc.scalar.activation(q_to, ps, ACT.Copy, scale=rstd[:, t:t + 1])
                    i = nc.scalar.activation(s_to, ps, ACT.Square, scale=rstd[:, t:t + 1])
                i.then_inc(qk_read, 1)

            def read_vals(c, bank, at=0, width=CW):
                act.wait_ge(visit_done, (c + 1) * V)
                for t in range(T):
                    i = nc.scalar.activation(vals[:, t, 0:width], ps_proj[2 * bank + t][:, at:at + width],
                                             ACT.Copy, scale=rstd[:, t:t + 1])
                i.then_inc(vals_ready, 1)

            def read_gate(c, bank):
                act.wait_ge(visit_done, (c + 1) * V)
                for t in range(T):
                    own.did(nc.scalar.activation(sq[:, t, :], ps_proj[2 * bank + t][:, :], ACT.Exp, scale=nrstd[:, t:t + 1]))

            def sigmoid():
                own.settle()
                own.did(nc.scalar.activation(sq[:, :, :], sq[:, :, :], ACT.Ln, bias=one_c))
                own.settle()
                nc.scalar.activation(sq[:, :, :], sq[:, :, :], ACT.Exp, scale=-1.0).then_inc(sig_ready, 1)

            def move_qkT(step, half, to):
                act.wait_ge(qk_flipped, step + 1)
                nc.scalar.activation(to[:, 2 * half:2 * half + 2, :].rearrange("p b n -> p (b n)"), ps_t[:, :], ACT.Copy)\
                    .then_inc(qkT_ready, 1)

            def exp_scores(n, j, odd):
                act.wait_ge(max_ready, n + 1)
                for a in range(2 if odd else 1):
                    for t in range(T):
                        r = (slice(0, P), slice(P, 3 * P))[t]
                        i = nc.scalar.activation(prob[:, j % 2, a, r], prob[:, j % 2, a, r], ACT.Exp,
                                                 bias=negmax[:, j % 2, a, t:t + 1], accum_out=rowsum[:, j % 2, a, t:t + 1])
                if odd:
                    i = nc.scalar.activation(esink[:, j % 2, :, :], sinkdiff[:, j % 2, :, :], ACT.Exp)
                i.then_inc(prob_ready, 1)

            def move_probT(n, j, odd):
                act.wait_ge(prob_flipped, n + 1)
                for a in range(2 if odd else 1):
                    i = nc.scalar.activation(probT[:, a, :], (ps_p, ps_s)[a][:, 0:3 * P], ACT.Copy)
                i.then_inc(probT_ready, 1)

            def y_hi_part(n, kt):
                act.wait_ge(y_flipped, n + 1)
                nc.scalar.activation(y_hi[:, kt, :], ps_o[:, 2 * P:4 * P], ACT.Copy).then_inc(yhi_ready, 1)

            def attention(h, base, kt, odd, stages=BESIDE):
                at = stages[odd]
                for j in range(4):
                    if h == at[3][j]:
                        y_hi_part(base + j, kt + j)
                for j in range(4):
                    if h == at[1][j]:
                        move_probT(base + j, j, odd)
                for j in range(4):
                    if h == at[0][j] + 1:
                        exp_scores(base + j, j, odd)

            def output_stage(layer):
                c0 = OUT1 if layer else OUT0
                for v in range(len(OUT_ORDER)):
                    if not (layer and v >= len(OUT_ORDER) - LEAD):
                        ahead(c0 + v // V, v % V)
                    if v == 0:
                        read_gate(c0 - 1, (c0 - 1) % 2)
                    if v == 2 - layer:
                        sigmoid()
                    if layer and v == 0:
                        act.wait_ge(sinks_picked, 4)
                    if v < 14:
                        attention(v, 16 * layer + 12, 12, layer == 1, AT_END)
                    if layer == 0:
                        for c, at in enumerate((20, 23, 29)):
                            if v == at:
                                x_hi_part(1, c)
                                squares(1, c)

            for to, src in ((qT[0:KT, 0, 0:P], norm_even[0].rearrange("(k p) -> k p", p=P)),
                            (qT[KT:2 * KT, 0, 0:P], norm_odd[0].rearrange("(k p) -> k p", p=P))):
                act.dma_start(to, src).then_inc(norms_landed, 16)
            act.preload_act_table_set("natural_log_exp_and_others")
            act.wait_ge(norms_flipped, 1)
            nc.scalar.activation(norms[:, :], ps_proj[3][:, 0:2 * KT], ACT.Copy).then_inc(norms_ready, 1)
            act.wait_ge(norms_ready, 1)
            split_hi(0, 0, IW)
            x_hi_part(0, 0)
            for s in range(1, LEAD):
                split_hi(0, s, IW)
            squares(0, 0)
            for c in range(GROUP0):
                for s in range(V):
                    ahead(c, s, chunk_width(c + 1))
                    if c == 0 and s in (0, 2, 4):
                        x_hi_part(0, s // 2 + 1)
                        squares(0, s // 2 + 1)
                    if c == 0 and s == 4:
                        root(event_of("rstd0"), T)
                    if c >= 1 and s == 0:
                        read_index(c - 1)

            for part in range(4):
                for s in range(V):
                    h = V * part + s
                    ahead(GROUP0 + part, s)
                    if h == 0:
                        read_index(2)
                        root(event_of("ik"), T)
                        act.wait_ge(gate_abs, 1)
                        own.did(nc.scalar.activation(ezf, azf, ACT.Exp, scale=-1.0))
                        own.settle()
                        nc.scalar.activation(lzf, ezf, ACT.Ln, bias=one_c).then_inc(gate_soft, 1)
                    if 5 <= h < 9:
                        act.wait_ge(ix_flipped, h - 4)
                        nc.scalar.activation(ixT[:, 2 * (h - 5):2 * (h - 5) + 2, :].rearrange("p b n -> p (b n)"),
                                             (ps_s, ps_t, ps_p, ps_o)[h - 5][:, :], ACT.Copy).then_inc(ixT_ready, 1)
                    if h == 9:
                        act.wait_ge(ix_flipped, 5)
                        nc.scalar.activation(ikT[:, :], ps_t[:, 0:2 * P], ACT.Copy).then_inc(ixT_ready, 1)
                    if h == V:
                        read_qk(GROUP0, GROUP0 % 2, CW, 0, None)
                    if h == V + 2:
                        root(event_of("even", 0), 8)
                    if 11 <= h < 19:
                        i = h - 11
                        act.wait_ge(logits_done, i + 1)
                        if i >= 2:
                            act.wait_ge(weighed, i - 1)
                        for a, bank in enumerate((ps_s, ps_p)):
                            r = nc.scalar.activation(prob[:, i % 2, a, :], bank[:, 0:3 * P], ACT.Relu, scale=ID ** -0.5)
                        r.then_inc(relu_ready, 1)
                    if h in (14, 15):
                        move_qkT(h - 14, h - 14, qT)
                    if h == 2 * V:
                        read_qk(GROUP0 + 1, (GROUP0 + 1) % 2, CW, 1, None)
                    if h == 2 * V + 2:
                        root(event_of("even", 1), 8)
                    if h in (27, 28):
                        move_qkT(h - 25, h - 27, kT)
                    if h == 3 * V:
                        read_vals(GROUP0 + 2, (GROUP0 + 2) % 2)
            with act.Fori(0, 3) as turn:
                own.enter(turn, 5)
                c0 = turn * 4 + GROUP0 + 4
                for part in range(4):
                    for s in range(V):
                        h = V * part + s
                        ahead(c0 + part, s)
                        if h == 0:
                            read_gate(c0 - 1, (GROUP0 + 3) % 2)
                        if h == 2:
                            sigmoid()
                        attention(h, turn * 4, turn * 4, False)
                        if h == V:
                            read_qk(c0, GROUP0 % 2, CW, turn * 2 + 2, turn + 1)
                        if h == V + 2:
                            root(turn * 2 + event_of("even", 2), 8)
                        if h in (15, 16):
                            move_qkT(turn * 4 + 4 + h - 15, h - 15, qT)
                        if h == 2 * V + 1:
                            read_qk(c0 + 1, (GROUP0 + 1) % 2, CW, turn * 2 + 3, None)
                        if h == 2 * V + 3:
                            root(turn * 2 + event_of("even", 3), 8)
                        if h in (23, 24):
                            move_qkT(turn * 4 + 6 + h - 23, h - 23, kT)
                        if h == 3 * V:
                            read_vals(c0 + 2, (GROUP0 + 2) % 2)
                own.leave(3)
            output_stage(0)

            for s in range(V):
                ahead(KV, s)
                if s == 3:
                    x_hi_part(1, 3)
                    squares(1, 3)
                    root(event_of("rstd1"), T)
            for part in range(2):
                for s in range(V):
                    h = V * part + s
                    ahead(SWA0 + part, s)
                    if h == 0:
                        act.wait_ge(rstd_ready, 2)
                        read_qk(KV, KV % 2, SKV * SD, 8, 4)
                        read_vals(KV, KV % 2, SKV * SD, SKV * SD)
                    if h == 2:
                        root(event_of("kv"), 8)
                    if h in (5, 6):
                        move_qkT(16 + h - 5, h - 5, kT)
                    if h == V:
                        read_qk(SWA0, 0, CW, 9, None)
                    if h == V + 2:
                        root(event_of("odd", 0), 16)
                    if h in (13, 15):
                        move_qkT(18 + (h - 13) // 2, (h - 13) // 2, qT)
            with act.Fori(0, 3) as turn:
                own.enter(turn, 4)
                c0 = turn * 2 + SWA0 + 2
                for part in range(2):
                    for s in range(V):
                        h = V * part + s
                        ahead(c0 + part, s)
                        if h == 0:
                            read_gate(c0 - 1, 1)
                        if h == 2:
                            sigmoid()
                        if h == 0:
                            act.wait_ge(sinks_picked, turn + 1)
                        attention(h, turn * 4 + 16, turn * 4, True)
                        if h == V + 1:
                            read_qk(c0, 0, CW, turn + 10, turn + 5)
                        if h == V + 2:
                            root(turn + event_of("odd", 1), 16)
                        if h in (14, 15):
                            move_qkT(turn * 2 + 20 + h - 14, h - 14, qT)
                own.leave(3)
            output_stage(1)

        @block.vector
        def _(dve):
            own = Steps(dve, dve_did)
            v_ = nc.vector

            def split_lo(c, s, width=CW):
                dve.wait_ge(hi_ready, V * c + s + 1)
                v_.tensor_tensor(w_lo[:, s % HL, :, 0:width], w_raw[:, s % RAW, :, 0:width],
                                 w_hi[:, s % HL, :, 0:width], ALU.subtract).then_inc(lo_ready, 1)

            def ahead(c, s, next_width=CW):
                if s < V - LEAD:
                    split_lo(c, s + LEAD, chunk_width(c))
                else:
                    split_lo(c + 1, s + LEAD - V, next_width)

            def x_lo_part(layer, c):
                banks = (ps_s, ps_t) if c % 2 == 0 else (ps_p, ps_o)
                for k in range(4):
                    kt = 4 * c + k
                    if k % 2 == 0:
                        dve.wait_ge(xhi_ready, V * layer + 2 * c + k // 2 + 1)
                    i = v_.scalar_tensor_tensor(out=x_lo[:, kt, :], in0=banks[k // 2][:, (k % 2) * 2 * P:(k % 2 + 1) * 2 * P],
                                                scalar=norms[:, KT * layer + kt:KT * layer + kt + 1],
                                                in1=x_hi[:, kt, :], op0=ALU.mult, op1=ALU.subtract)
                    if k % 2:
                        i.then_inc(xlo_ready, 1)

            def variance(ss, n, count):
                own.settle()
                v_.tensor_scalar(var[:, 0:n], ss, 1.0 / count, EPS, ALU.mult, ALU.add).then_inc(var_ready, 1)

            def refine(e, n, to):
                dve.wait_ge(var_ready, e + 1)
                dve.wait_ge(root_ready, e + 1)
                own.did(v_.tensor_tensor(na[:, 0:n], r0[:, 0:n], r0[:, 0:n], ALU.mult))
                own.settle()
                own.did(v_.tensor_tensor(nb[:, 0:n], na[:, 0:n], var[:, 0:n], ALU.mult))
                own.settle()
                own.did(v_.tensor_scalar(na[:, 0:n], nb[:, 0:n], -0.5, 1.5, ALU.mult, ALU.add))
                own.settle()
                own.did(v_.tensor_tensor(to, na[:, 0:n], r0[:, 0:n], ALU.mult))
                own.settle()

            def stream_rstd(layer):
                dve.wait_ge(squares_ready, OC * (layer + 1))
                own.did(v_.tensor_reduce(ssum, ssq, AX.X, ALU.add))
                variance(ssum, T, D)
                refine(event_of(f"rstd{layer}"), T, rstd)
                v_.tensor_scalar(nrstd, rstd, -1.0, None, ALU.mult).then_inc(rstd_ready, 1)

            def heads(buf, nh, dh):
                return buf[:, :, :].rearrange("p t n -> p (t n)")[:, 0:T * nh * dh].rearrange("p (h d) -> p h d", d=dh)

            def per_tile(buf, nh, dh):
                return buf[:, :, :].rearrange("p t n -> p (t n)")[:, 0:T * nh * dh].rearrange("p (t h d) -> p t h d", t=T, d=dh)

            def qk_variance(k, nh, dh):
                dve.wait_ge(qk_read, k + 1)
                own.did(v_.tensor_reduce(ssumq[:, 0:T * nh], heads(sq, nh, dh), AX.X, ALU.add))
                variance(ssumq[:, 0:T * nh], T * nh, dh)

            def qk_norm(e, nh, dh):
                n = T * nh
                refine(e, n, rinv[:, 0:n])
                h = heads(qk, nh, dh)
                v_.tensor_tensor(h, h, rinv[:, 0:n].unsqueeze(2).to_broadcast([P, n, dh]), ALU.mult).then_inc(qk_normed, 1)

            def qk_cos(k, nh, dh, table):
                dve.wait_ge(qk_normed, k + 1)
                own.did(v_.tensor_tensor(per_tile(tmp, nh, dh), per_tile(qk, nh, dh),
                                         table.unsqueeze(2).to_broadcast([P, T, nh, dh]), ALU.mult))

            def qk_rope(k, nh, dh, twice=False):
                dve.wait_ge(qk_swapped, k + 1)
                own.settle()
                if twice:
                    to = qk[:, :, :].rearrange("p t (h a d) -> p t h a d", a=2, d=dh)
                    own.did(v_.tensor_tensor(to[:, :, :, 0, :], per_tile(tmp, nh, dh), per_tile(sq, nh, dh), ALU.add))
                    v_.tensor_tensor(to[:, :, :, 1, :], per_tile(tmp, nh, dh), per_tile(sq, nh, dh), ALU.add)\
                        .then_inc(qk_ready, 1)
                else:
                    v_.tensor_tensor(heads(qk, nh, dh), heads(tmp, nh, dh), heads(sq, nh, dh), ALU.add).then_inc(qk_ready, 1)

            def make_gate(k, bank):
                dve.wait_ge(sig_ready, k + 1)
                for t in range(T):
                    i = v_.scalar_tensor_tensor(out=gate[:, t, :], in0=ps_proj[2 * bank + t][:, :], scalar=rstd[:, t:t + 1],
                                                in1=sq[:, t, :], op0=ALU.mult, op1=ALU.mult)
                i.then_inc(gate_ready, 1)
                dve.wait_ge(gate_ready, k + 1)

            def shift_scores_even(n, j, slot):
                dve.wait_ge(scores_done, n + 1)
                own.did(v_.tensor_tensor(prob[:, j % 2, 0, :], ps_s[:, 0:3 * P], bias[:, slot, :], ALU.subtract))
                own.settle()
                v_.tensor_reduce(negmax[:, j % 2, 0, 0:1], prob[:, j % 2, 0, 0:P], AX.X, ALU.max, negate=True)
                v_.tensor_reduce(negmax[:, j % 2, 0, 1:2], prob[:, j % 2, 0, P:3 * P], AX.X, ALU.max, negate=True)\
                    .then_inc(max_ready, 1)

            def shift_scores_odd(n, j):
                dve.wait_ge(consts_ready, 2)
                dve.wait_ge(scores_done, n + 1)
                own.did(v_.tensor_copy(spare, sink_now[:, 0:1]))
                for a, bank in enumerate((ps_s, ps_t)):
                    for t, r in enumerate((slice(0, P), slice(P, 3 * P))):
                        own.did(v_.tensor_tensor_reduce(prob[:, j % 2, a, r], bank[:, r], mask[:, r], 1.0,
                                                        sink_now[:, 2 * j + a:2 * j + a + 1], ALU.subtract, ALU.max,
                                                        rowmax[:, j % 2, a, t:t + 1]))
                own.settle()
                own.did(v_.tensor_tensor(sinkdiff[:, j % 2, :, :],
                                         sink_now[:, 2 * j:2 * j + 2].unsqueeze(2).to_broadcast([P, 2, T]),
                                         rowmax[:, j % 2, :, :], ALU.subtract))
                v_.tensor_scalar(negmax[:, j % 2, :, :], rowmax[:, j % 2, :, :], -1.0, None, ALU.mult).then_inc(max_ready, 1)

            def make_y(n, j, odd):
                dve.wait_ge(prob_ready, n + 1)
                dve.wait_ge(pv_done, n + 1)
                na_ = 2 if odd else 1
                if odd:
                    own.did(v_.tensor_tensor(rowsum[:, j % 2, :, :], rowsum[:, j % 2, :, :], esink[:, j % 2, :, :], ALU.add))
                    own.settle()
                own.did(v_.reciprocal(rsum[:, 0:na_, :], rowsum[:, j % 2, 0:na_, :]))
                own.settle()
                w = P // na_
                for a in range(na_):
                    for t in range(T):
                        o = a * w
                        i = v_.scalar_tensor_tensor(out=ysb[:, j % 2, t, o:o + w], in0=ps_o[:, t * P + o:t * P + o + w],
                                                    scalar=rsum[:, a, t:t + 1], in1=gate[:, t, j * P + o:j * P + o + w],
                                                    op0=ALU.mult, op1=ALU.mult)
                i.then_inc(y_ready, 1)

            def y_lo_part(n, kt):
                dve.wait_ge(yhi_ready, n + 1)
                v_.tensor_tensor(y_lo[:, kt, :], ps_o[:, 2 * P:4 * P], y_hi[:, kt, :], ALU.subtract).then_inc(ylo_ready, 1)

            def attention(h, base, slot, kt, odd, stages=BESIDE):
                at = stages[odd]
                for j in range(4):
                    if h == at[3][j]:
                        y_lo_part(base + j, kt + j)
                for j in range(4):
                    if h == at[2][j]:
                        make_y(base + j, j, odd)
                for j in range(4):
                    if h == at[0][j]:
                        if odd:
                            shift_scores_odd(base + j, j)
                        else:
                            shift_scores_even(base + j, j, slot(j))

            def pick_sinks(group):
                v_.tensor_copy(sink_now, sinks_b[:, bass.ds(group * 8, 8)]).then_inc(sinks_picked, 1)
                dve.wait_ge(sinks_picked, group + 1)

            def add_output(layer, c, done):
                dve.wait_ge(visit_done, done)
                if layer == 0 and c == 0:
                    dve.wait_ge(resid_landed, 16 * OC)
                for t in range(T):
                    if (layer, c, t) == (1, OC - 1, 1):
                        i.then_inc(out_added, 1)
                        dve.wait_ge(visit_done, done + 1)
                    r = resid[:, t, c * CW:(c + 1) * CW]
                    i = v_.tensor_tensor(r, ps_proj[2 * ((OUT1 if layer else OUT0) + c) % 4 + t][:, :], r, ALU.add)
                i.then_inc(out_added, 1)

            def output_stage(layer):
                c0 = OUT1 if layer else OUT0
                if layer:
                    pick_sinks(3)
                    attention(-1, 28, None, 12, True, AT_END)
                for v in range(len(OUT_ORDER)):
                    for c, at in enumerate((15, 16, 24)):
                        if v == at:
                            add_output(layer, c, V * c0 + at)
                    if not (layer and v >= len(OUT_ORDER) - LEAD):
                        ahead(c0 + v // V, v % V)
                    if v == 3 - layer:
                        make_gate(3 + 4 * layer, (c0 - 1) % 2)
                    if v < 14:
                        attention(v, 16 * layer + 12, lambda j: H0, 12, layer == 1, AT_END)
                    if layer == 0:
                        for c, at in enumerate((20, 23, 29)):
                            if v == at:
                                x_lo_part(1, c)

            split_lo(0, 0, IW)
            x_lo_part(0, 0)
            for s in range(1, LEAD):
                split_lo(0, s, IW)
            for c in range(GROUP0):
                for s in range(V):
                    ahead(c, s, chunk_width(c + 1))
                    if c == 0 and s in (0, 2, 4):
                        x_lo_part(0, s // 2 + 1)
                    if c == 0 and s == 4:
                        stream_rstd(0)

            ik = ix[:, :, IK:IK + ID]
            iw = ix[:, :, IWT:IWT + IH]
            ROUND0 = 22
            for part in range(4):
                for s in range(V):
                    h = V * part + s
                    ahead(GROUP0 + part, s)
                    if h == 0:
                        dve.wait_ge(chunk_read, 3)
                        dve.wait_ge(consts_ready, 2)
                        dve.wait_ge(tables_ready, 1)
                        dve.wait_ge(small_landed, N_SMALL)
                        own.did(v_.tensor_tensor(ikn[:, :, 0, :], ik, ik, ALU.mult))
                        own.settle()
                        own.did(v_.tensor_reduce(ssumq[:, 0:T], ikn[:, :, 0, :], AX.X, ALU.add))
                        variance(ssumq[:, 0:T], T, ID)
                        own.did(v_.tensor_tensor(zf, ix[:, :, IAF:IAF + H0], bf_b.unsqueeze(1).to_broadcast([P, T, H0]), ALU.add))
                        own.settle()
                        own.did(v_.tensor_scalar(nzf, zf, -1.0, None, ALU.mult))
                        own.settle()
                        v_.tensor_tensor(azf, zf, nzf, ALU.max).then_inc(gate_abs, 1)
                        own.did(v_.tensor_scalar(mzf, zf, 0.0, None, ALU.min))
                        own.did(v_.tensor_scalar(iw, iw, IH ** -0.5, None, ALU.mult))
                        refine(event_of("ik"), T, rinv[:, 0:T])
                        for t in range(T):
                            i = v_.tensor_scalar(ikn[:, t, 1, :], ik[:, t, :], rinv[:, t:t + 1], None, ALU.mult)
                            own.did(i)
                        own.settle()
                        v_.tensor_tensor(ikn[:, :, 2, :], ikn[:, :, 1, :], tab64_c[:, 1, :, :], ALU.mult).then_inc(ik_read, 1)
                        dve.wait_ge(gate_soft, 1)
                        v_.tensor_tensor(logf, mzf, lzf, ALU.subtract).then_inc(logf_ready, 1)
                    if h == 1:
                        dve.wait_ge(logf_ready, 1)
                        for b in range(2):
                            i = v_.tensor_copy(lf_b[b], logf[:, :, 4 * b:4 * b + 4].unsqueeze(3).to_broadcast([P, T, 4, P]))
                        i.then_inc(lfb_ready, 1)
                    if h == 2:
                        dve.wait_ge(ik_read, 1)
                        dve.wait_ge(ik_swapped, 1)
                        own.did(v_.tensor_tensor(ikn[:, :, 3, :], ikn[:, :, 2, :], ikn[:, :, 0, :], ALU.add))
                        own.settle()
                        v_.tensor_copy(ikn[:, :, 2, :], ikn[:, :, 3, :]).then_inc(ix_roped, 1)
                    if h in (2, 3):
                        t = h - 2
                        q = ix[:, t, 0:IH * ID].rearrange("p (h d) -> p h d", d=ID)
                        m = tmp[:, :, :].rearrange("p t n -> p (t n)").rearrange("p (h d) -> p h d", d=ID)
                        w = (sq, qk)[t][:, :, :].rearrange("p t n -> p (t n)").rearrange("p (h d) -> p h d", d=ID)
                        if t == 1:
                            dve.wait_ge(ix_roped, 2)
                        own.did(v_.tensor_tensor(m, q, tab64_c[:, 0, t, :].unsqueeze(1).to_broadcast([P, IH, ID]), ALU.mult))
                        own.settle()
                        dve.wait_ge(ix_swapped, t + 1)
                        v_.tensor_tensor(q, m, w, ALU.add).then_inc(ix_roped, 1)
                    if h == 4:
                        dve.wait_ge(cq_done, 1)
                        v_.tensor_copy(cq, ps_o[:, 0:2 * H0].rearrange("p (t h) -> p t h", t=T)).then_inc(cq_ready, 1)
                        dve.wait_ge(cq_ready, 1)
                    if h == V + 2:
                        qk_variance(0, 4, HD)
                    if 10 <= h < 14:
                        i0 = h - 10
                        dve.wait_ge(ck_done, i0 + 1)
                        for b in range(2):
                            hh = 2 * i0 + b
                            ck = ps_o[:, b * 2 * P:(b + 1) * 2 * P]
                            v_.scalar_tensor_tensor(out=bias[:, hh, 0:P], in0=ck[:, 0:P], scalar=cq[:, 0, hh:hh + 1],
                                                    in1=mask[:, 0:P], op0=ALU.subtract, op1=ALU.add)
                            v_.tensor_scalar(bias[:, hh, P:2 * P], ck[:, 0:P], cq[:, 1, hh:hh + 1], None, ALU.subtract)
                            i = v_.scalar_tensor_tensor(out=bias[:, hh, 2 * P:3 * P], in0=ck[:, P:2 * P],
                                                        scalar=cq[:, 1, hh:hh + 1], in1=mask[:, 2 * P:3 * P],
                                                        op0=ALU.subtract, op1=ALU.add)
                        i.then_inc(ck_read, 1)
                    if h == V + 3:
                        qk_norm(event_of("even", 0), 4, HD)
                    if h == V + 4:
                        qk_cos(0, 4, HD, tab_c[:, 0])
                    if h == V + 5:
                        qk_rope(0, 4, HD)
                    if 11 <= h < 19:
                        i0 = h - 11
                        dve.wait_ge(relu_ready, i0 + 1)
                        for a in range(2):
                            hh = 2 * i0 + a
                            own.settle()
                            if a == 0 and i0:
                                dve.wait_ge(weighed, i0)
                            for t, r in enumerate((slice(0, P), slice(P, 3 * P))):
                                if hh == 0:
                                    i = v_.tensor_scalar(score[:, r], prob[:, 0, 0, r], iw[:, t, 0:1], None, ALU.mult)
                                else:
                                    i = v_.scalar_tensor_tensor(out=score[:, r], in0=prob[:, i0 % 2, a, r],
                                                                scalar=iw[:, t, hh:hh + 1], in1=score[:, r],
                                                                op0=ALU.mult, op1=ALU.add)
                                if a == 0:
                                    own.did(i)
                        i.then_inc(weighed, 1)
                    if h == 2 * V + 2:
                        qk_variance(1, 4, HD)
                    if h == 2 * V + 3:
                        qk_norm(event_of("even", 1), 4, HD)
                    if h == 2 * V + 4:
                        qk_cos(1, 4, HD, tab_c[:, 1])
                    if h == 2 * V + 5:
                        qk_rope(1, 4, HD)
                    if h == 19:
                        dve.wait_ge(weighed, 8)
                        own.did(v_.tensor_tensor(score[:, 0:P], score[:, 0:P], mask[:, 0:P], ALU.subtract))
                        v_.tensor_tensor(score[:, 2 * P:3 * P], score[:, 2 * P:3 * P], mask[:, 2 * P:3 * P], ALU.subtract)\
                            .then_inc(weighed, 1)
                        dve.wait_ge(weighed, 9)
                    if ROUND0 <= h < ROUND0 + TOPK // 8:
                        tiles = (slice(0, P), slice(P, 3 * P))
                        for t, r in enumerate(tiles):
                            i = v_.max(top8[:, t, :], score[:, r])
                            own.did(i)
                        own.settle()
                        for t, r in enumerate(tiles):
                            i = v_.match_replace(score[:, r], top8[:, t, :], score[:, r], TAKEN)
                            if t == 0:
                                own.did(i)
                        i.then_inc(weighed, 1)
                        own.settle()
                        dve.wait_ge(weighed, 10 + h - ROUND0)
                    if h == ROUND0 + TOPK // 8:
                        own.did(v_.tensor_scalar(bias[:, H0, :], score[:, :], TAKEN / 2, MASKED, ALU.is_gt, ALU.mult))
                        own.settle()
                        own.did(v_.tensor_tensor(bias[:, H0, 0:P], bias[:, H0, 0:P], mask[:, 0:P], ALU.max))
                        v_.tensor_tensor(bias[:, H0, 2 * P:3 * P], bias[:, H0, 2 * P:3 * P], mask[:, 2 * P:3 * P],
                                         ALU.max).then_inc(weighed, 1)
            dve.wait_ge(ck_read, 4)
            dve.wait_ge(weighed, 18)
            with dve.Fori(0, 3) as turn:
                own.enter(turn, 20)
                c0 = turn * 4 + GROUP0 + 4
                kind = (turn + 1) >> 1
                for part in range(4):
                    for s in range(V):
                        h = V * part + s
                        ahead(c0 + part, s)
                        if h == 3:
                            make_gate(turn, (GROUP0 + 3) % 2)
                        attention(h, turn * 4, lambda j: turn * 4 + j - (turn >> 1) * j, turn * 4, False)
                        for b in range(2):
                            if h == (1 + b) * V + 1 + b:
                                qk_variance(turn * 2 + 2 + b, 4, HD)
                            if h == (1 + b) * V + 2 + b:
                                qk_norm(turn * 2 + event_of("even", 2 + b), 4, HD)
                            if h == (1 + b) * V + 4:
                                qk_cos(turn * 2 + 2 + b, 4, HD, tab_c[:, kind * 2 + b])
                            if h == (1 + b) * V + 6:
                                qk_rope(turn * 2 + 2 + b, 4, HD)
                own.leave(3)
            output_stage(0)

            for s in range(V):
                ahead(KV, s)
                if s == 0:
                    add_output(0, 3, V * KV)
                if s == 3:
                    x_lo_part(1, 3)
                    stream_rstd(1)
            for part in range(2):
                for s in range(V):
                    h = V * part + s
                    ahead(SWA0 + part, s)
                    if h == 1:
                        qk_variance(8, SKV, SD)
                    if h == 2:
                        qk_norm(event_of("kv"), SKV, SD)
                    if h == 3:
                        qk_cos(8, SKV, SD, tab64_c[:, 3])
                    if h == 4:
                        qk_rope(8, SKV, SD, twice=True)
                    if h == V + 1:
                        qk_variance(9, 8, SD)
                    if h == V + 2:
                        qk_norm(event_of("odd", 0), 8, SD)
                    if h == V + 3:
                        qk_cos(9, 8, SD, tab64_c[:, 2])
                    if h == V + 4:
                        qk_rope(9, 8, SD)
            with dve.Fori(0, 3) as turn:
                own.enter(turn, 38)
                c0 = turn * 2 + SWA0 + 2
                for part in range(2):
                    for s in range(V):
                        h = V * part + s
                        ahead(c0 + part, s)
                        if h == 0:
                            pick_sinks(turn)
                        if h == 3:
                            make_gate(turn + 4, 1)
                        attention(h, turn * 4 + 16, None, turn * 4, True)
                        if h == V + 1:
                            qk_variance(turn + 10, 8, SD)
                        if h == V + 2:
                            qk_norm(turn + event_of("odd", 1), 8, SD)
                        if h == V + 3:
                            qk_cos(turn + 10, 8, SD, tab64_c[:, 2])
                        if h == V + 5:
                            qk_rope(turn + 10, 8, SD)
                own.leave(3)
            output_stage(1)
            add_output(1, 3, V * NCH)

        @block.gpsimd
        def _(pool):
            own = Steps(pool, pool_did)
            g = nc.gpsimd
            own.did(g.memset(ident[:, :], 1.0))
            own.settle()
            g.affine_select(out=ident[:, :], in_=ident[:, :], pattern=[[-1, P]], compare_op=ALU.is_equal, fill=0.0,
                            base=0, channel_multiplier=1).then_inc(consts_ready, 1)
            own.did(g.memset(tri, 1.0))
            own.did(g.memset(mask[:, :], 0.0))
            own.settle()
            g.memset(one_c, 1.0)
            own.did(g.affine_select(out=tri[:, 0:P], in_=tri[:, 0:P], pattern=[[1, P]], compare_op=ALU.is_ge, fill=0.0,
                                    base=0, channel_multiplier=-1))
            for b in (0, 2):
                own.did(g.affine_select(out=mask[:, b * P:(b + 1) * P], in_=mask[:, b * P:(b + 1) * P], pattern=[[-1, P]],
                                        compare_op=ALU.is_ge, fill=MASKED, base=0, channel_multiplier=1))
            g.affine_select(out=mask[:, P:2 * P], in_=mask[:, P:2 * P], pattern=[[1, P]],
                            compare_op=ALU.is_gt, fill=MASKED, base=0, channel_multiplier=-1).then_inc(consts_ready, 1)
            for to, src in ((rope_sb, rope_dram),
                            (gains[:, 0:2 * HD], g_qk_fox.rearrange("a b d -> a (b d)")[0].partition_broadcast(P)),
                            (gains[:, 2 * HD:4 * HD], g_qk_dsa.rearrange("a b d -> a (b d)")[0].partition_broadcast(P)),
                            (gains[:, 4 * HD:4 * HD + ID], g_kidx[0].partition_broadcast(P)),
                            (gains[:, 4 * HD + ID:4 * HD + ID + 2 * SD],
                             g_qk_swa.rearrange("a b d -> a (b d)")[0].partition_broadcast(P)),
                            (sinks_b, sinks[0].partition_broadcast(P)),
                            (bf_b, b_f_even[0].partition_broadcast(P))):
                pool.dma_start(to, src).then_inc(small_landed, 16)
            pool.wait_ge(small_landed, N_SMALL)
            for at in (0, 2 * HD, 4 * HD + ID):
                w = HD if at < 4 * HD else SD
                own.did(g.tensor_scalar(gains[:, at:at + w], gains[:, at:at + w], w ** -0.5, None, ALU.mult))
            own.settle()

            def table(tc, ts, at, dh, rope_at, roped=True, gained=True, signal=None):
                half = dh // 2
                if not roped:
                    own.did(g.tensor_copy(tc, gains[:, at:at + dh].unsqueeze(1).to_broadcast([P, T, dh])))
                    own.did(g.memset(ts, 0.0))
                    return
                cos, sin = rope_sb[:, :, rope_at:rope_at + half], rope_sb[:, :, rope_at + half:rope_at + dh]
                lo, hi = slice(0, half), slice(half, dh)
                if not gained:
                    own.did(g.tensor_copy(tc[:, :, lo], cos))
                    own.did(g.tensor_copy(tc[:, :, hi], cos))
                    own.did(g.tensor_scalar(ts[:, :, lo], sin, -1.0, None, ALU.mult))
                    own.did(g.tensor_copy(ts[:, :, hi], sin))
                    return
                g1 = gains[:, at:at + half].unsqueeze(1).to_broadcast([P, T, half])
                g2 = gains[:, at + half:at + dh].unsqueeze(1).to_broadcast([P, T, half])
                own.did(g.tensor_tensor(tc[:, :, lo], cos, g1, ALU.mult))
                own.did(g.tensor_tensor(tc[:, :, hi], cos, g2, ALU.mult))
                own.did(g.tensor_tensor(ts[:, :, lo], sin, g2, ALU.mult))
                own.did(g.tensor_tensor(ts[:, :, hi], sin, g1, ALU.mult))
                own.settle()
                last = g.tensor_scalar(ts[:, :, lo], ts[:, :, lo], -1.0, None, ALU.mult)
                own.did(last) if signal is None else last.then_inc(signal, 1)

            table(tab64_c[:, 0], tab64_s[:, 0], 0, ID, HD, gained=False)
            table(tab64_c[:, 1], tab64_s[:, 1], 4 * HD, ID, HD)
            table(tab64_c[:, 2], tab64_s[:, 2], 4 * HD + ID, SD, HD)
            table(tab64_c[:, 3], tab64_s[:, 3], 4 * HD + 2 * ID, SD, HD)
            table(tab_c[:, 0], tab_s[:, 0], 0, HD, 0, roped=False)
            table(tab_c[:, 1], tab_s[:, 1], HD, HD, 0, roped=False)
            table(tab_c[:, 2], tab_s[:, 2], 2 * HD, HD, 0)
            table(tab_c[:, 3], tab_s[:, 3], 3 * HD, HD, 0, signal=tables_ready)
            own.settle()
            pool.wait_ge(tables_ready, 1)

            pool.wait_ge(chunk_read, 3)
            half = ID // 2
            for t in range(T):
                q = ix[:, t, 0:IH * ID].rearrange("p (h d) -> p h d", d=ID)
                w = (sq, qk)[t][:, :, :].rearrange("p t n -> p (t n)").rearrange("p (h d) -> p h d", d=ID)
                for a, b in ((0, half), (half, 0)):
                    s_ = tab64_s[:, 0, t, a:a + half].unsqueeze(1).to_broadcast([P, IH, half])
                    i = g.tensor_tensor(w[:, :, a:a + half], q[:, :, b:b + half], s_, ALU.mult)
                i.then_inc(ix_swapped, 1)
                if t == 0:
                    pool.wait_ge(ik_read, 1)
                    g.tensor_tensor(ikn[:, :, 0, 0:half], ikn[:, :, 1, half:ID], tab64_s[:, 1, :, 0:half], ALU.mult)
                    g.tensor_tensor(ikn[:, :, 0, half:ID], ikn[:, :, 1, 0:half], tab64_s[:, 1, :, half:ID], ALU.mult)\
                        .then_inc(ik_swapped, 1)

            def swap(k, nh, dh, table):
                pool.wait_ge(qk_normed, k + 1)
                h = dh // 2
                src = qk[:, :, :].rearrange("p t n -> p (t n)")[:, 0:T * nh * dh].rearrange("p (t h d) -> p t h d", t=T, d=dh)
                dst = sq[:, :, :].rearrange("p t n -> p (t n)")[:, 0:T * nh * dh].rearrange("p (t h d) -> p t h d", t=T, d=dh)
                g.tensor_tensor(dst[:, :, :, 0:h], src[:, :, :, h:dh],
                                table[:, :, 0:h].unsqueeze(2).to_broadcast([P, T, nh, h]), ALU.mult)
                g.tensor_tensor(dst[:, :, :, h:dh], src[:, :, :, 0:h],
                                table[:, :, h:dh].unsqueeze(2).to_broadcast([P, T, nh, h]), ALU.mult).then_inc(qk_swapped, 1)

            swap(0, 4, HD, tab_s[:, 0])
            swap(1, 4, HD, tab_s[:, 1])
            with pool.Fori(0, 3) as turn:
                kind = (turn + 1) >> 1
                for b in range(2):
                    swap(turn * 2 + 2 + b, 4, HD, tab_s[:, kind * 2 + b])
            swap(8, SKV, SD, tab64_s[:, 3])
            swap(9, 8, SD, tab64_s[:, 2])

            def pick(group):
                if not isinstance(group, int) or group >= 1:
                    pool.wait_ge(pv_done, group * 4 + 16)
                else:
                    pool.wait_ge(qkT_ready, 18)
                    pool.wait_ge(vals_ready, 5)
                g.tensor_copy(kT_now[:, :], kT[:, group, :]).then_inc(kv_picked, 1)
                g.tensor_copy(v_now[:, :, :], vals[:, :, bass.ds(group * SD, SD)]).then_inc(kv_picked, 1)

            pick(0)
            with pool.Fori(0, 3) as turn:
                swap(turn + 10, 8, SD, tab64_s[:, 2])
                pick(turn + 1)


_INS = ["x", "norm_even", "w_in_even", "b_f_even", "g_qk_fox", "g_qk_dsa", "g_kidx", "w_out_even",
        "norm_odd", "w_in_odd", "g_qk_swa", "sinks", "w_out_odd"]


def rope_constants(seq, dims=(128, 64), theta=10000.0):
    import numpy as np
    parts = []
    for dim in dims:
        inv = (np.float32(1.0) / np.float32(theta) ** (np.arange(0, dim, 2, dtype=np.float32) / np.float32(dim))).astype(np.float32)
        ang = (np.arange(seq, dtype=np.float32)[:, None] * inv[None, :]).astype(np.float32)
        parts += [np.cos(ang.astype(np.float64)), np.sin(ang.astype(np.float64))]
    return np.concatenate(parts, axis=1).astype(np.float32)


def kernel(**inputs):
    import numpy as _np
    import concourse.bacc as _bacc
    from concourse import mybir as _mybir
    from concourse.bass_utils import run_bass_kernel_spmd as _run

    nc = _bacc.Bacc("TRN2", target_bir_lowering=False, num_devices=1)
    arrays, args = {}, []
    for name in _INS:
        a = _np.ascontiguousarray(inputs[name])
        arrays[f"in_{name}"] = a
        args.append(nc.dram_tensor(f"in_{name}", a.shape, _mybir.dt.from_np(a.dtype), kind="ExternalInput").ap())
    shape = tuple(inputs["x"].shape)
    table = rope_constants(shape[1])
    arrays["rope_table"] = table
    args.append(nc.dram_tensor("rope_table", table.shape, _mybir.dt.float32, kind="ExternalInput").ap())
    args.append(nc.dram_tensor("out_0", shape, _mybir.dt.float32, kind="ExternalOutput").ap())
    hybrid_trunk(nc, *args)
    r = _run(nc, [arrays], core_ids=[0])
    return r.results[0]["out_0"]
```
